# Optimizing a Trainium2 kernel written in Bass

```python
import math
import jax, jax.numpy as jnp
from jax import lax
import numpy as np

D_MODEL = 1024
BATCH = 1
SEQ = 256
DEPTH = 2

GRID_W = 64
CTX_LEN = 256
ATTN_HEADS = 4
ATTN_HEAD_DIM = 64
ATTN_V_DIM = 2 * ATTN_HEAD_DIM
ATTN_WIDTH = ATTN_HEADS * ATTN_V_DIM
CONV_WIDTH = D_MODEL // 4
CONV_K = 3
POOL_WIDTH = D_MODEL // 4
POOL_WINDOWS = (2, 4, 8, 16)
POOL_GROUPS = len(POOL_WINDOWS)
POOL_GROUP_DIM = POOL_WIDTH // POOL_GROUPS
MIX_WIDTH = ATTN_WIDTH + CONV_WIDTH + POOL_WIDTH
D_FF = 2816
ROPE_BASE = 10000.0
Q_BLOCK = 128
N_MOD = 9
EPS = 1e-6
COL_SIZES = (ATTN_WIDTH, ATTN_WIDTH, ATTN_WIDTH, CONV_WIDTH, CONV_WIDTH, CONV_WIDTH, POOL_WIDTH)
COL_SPLITS = tuple(int(v) for v in np.cumsum(COL_SIZES)[:-1])
IN_COLS = sum(COL_SIZES)

kernel_name = "hymba_diffattn_conv_pool_macaron_dit"

def _rms(x, w):
    x32 = x.astype(jnp.float32)
    y = x32 * lax.rsqrt(jnp.mean(x32 * x32, axis=-1, keepdims=True) + EPS)
    return (y * w.astype(jnp.float32)).astype(x.dtype)

def _modulate(x, shift, scale):
    return x * (1 + scale[:, None, :]) + shift[:, None, :]

def _swiglu(x, w_gu, w_down):
    g, u = jnp.split(x @ w_gu, 2, axis=-1)
    return (jax.nn.silu(g) * u) @ w_down

def _axial_rope_tables(n_tokens):
    rows = n_tokens // GRID_W
    row = jnp.repeat(jnp.arange(rows), GRID_W).astype(jnp.float32)
    col = jnp.tile(jnp.arange(GRID_W), rows).astype(jnp.float32)
    nfreq = ATTN_HEAD_DIM // 4
    inv = ROPE_BASE ** (-jnp.arange(nfreq, dtype=jnp.float32) / nfreq)
    ang = jnp.stack([row[:, None] * inv, col[:, None] * inv], axis=1)
    return jnp.cos(ang), jnp.sin(ang)

def _apply_rope(x, cos, sin):
    xs = x.reshape(x.shape[:-1] + (2, 2, -1))
    x1, x2 = xs[..., 0, :], xs[..., 1, :]
    c = cos[None, :, None, None].astype(x.dtype)
    s = sin[None, :, None, None].astype(x.dtype)
    out = jnp.stack([x1 * c - x2 * s, x1 * s + x2 * c], axis=-2)
    return out.reshape(x.shape)

def _diff_attn(q, k, v, lam):
    s = jnp.einsum('bqhid,bkhid->bhiqk', q, k, preferred_element_type=jnp.float32)
    p = jax.nn.softmax(s * (ATTN_HEAD_DIM ** -0.5), axis=-1)
    a = p[:, :, 0] - lam * p[:, :, 1]
    return jnp.einsum('bhqk,bkhe->bqhe', a.astype(v.dtype), v)

def _diff_attn_blocked(q, k, v, lam):
    B, S = q.shape[:2]
    nb = S // Q_BLOCK
    qb = q.reshape((B, nb, Q_BLOCK) + q.shape[2:]).transpose(1, 0, 2, 3, 4, 5)
    out = lax.map(lambda qq: _diff_attn(qq, k, v, lam), qb)
    return out.transpose(1, 0, 2, 3, 4).reshape(B, S, ATTN_HEADS, ATTN_V_DIM)

def _attn_post(o, subln_w, lam_init):
    B, L = o.shape[:2]
    return (_rms(o, subln_w) * (1.0 - lam_init)).reshape(B, L, ATTN_WIDTH)

def _gated_conv(b, cg, xin, w):
    u = cg * xin
    L = u.shape[1]
    up = jnp.pad(u, ((0, 0), (1, 1), (0, 0)))
    return b * (up[:, :L] * w[0] + up[:, 1:L + 1] * w[1] + up[:, 2:] * w[2])

def _multiscale_pool(u, w_grp, scale):
    B, L, _ = u.shape
    ug = u.reshape(B, L, POOL_GROUPS, POOL_GROUP_DIM).astype(jnp.float32)
    csum = jnp.pad(jnp.cumsum(ug, axis=1), ((0, 0), (1, 0), (0, 0), (0, 0)))
    t = jnp.arange(L)
    outs = []
    for g, win in enumerate(POOL_WINDOWS):
        lo = jnp.clip(t - win // 2, 0, L)
        hi = jnp.clip(t + win // 2, 0, L)
        ssum = csum[:, hi, g] - csum[:, lo, g]
        cnt = (hi - lo).astype(jnp.float32)[None, :, None]
        outs.append(ssum / cnt - ug[:, :, g])
    pooled = jnp.stack(outs, axis=2).astype(u.dtype)
    y = jnp.einsum('blgc,gcd->blgd', pooled, w_grp).reshape(B, L, POOL_WIDTH)
    return y * scale

def _hybrid_mixer(u, uc, ctx_out, w_in, w_out, q_norm_w, k_norm_w, lam, lam_init,
                  subln_w, conv_w, pool_w, pool_scale, cos, sin):
    B, S, _ = u.shape
    Lc = uc.shape[1]
    H, dh = ATTN_HEADS, ATTN_HEAD_DIM
    if ctx_out:
        qc, kc, vc, cbc, ccc, cxc, puc = jnp.split(uc @ w_in, COL_SPLITS, axis=-1)
    else:
        kc, vc = jnp.split(uc @ w_in[:, ATTN_WIDTH:3 * ATTN_WIDTH], 2, axis=-1)
    kc = _rms(kc.reshape(B, Lc, H, 2, dh), k_norm_w)
    vc = vc.reshape(B, Lc, H, ATTN_V_DIM)
    q, k, v, cb, cc, cx, pu = jnp.split(u @ w_in, COL_SPLITS, axis=-1)
    q = _apply_rope(_rms(q.reshape(B, S, H, 2, dh), q_norm_w), cos, sin)
    k = _apply_rope(_rms(k.reshape(B, S, H, 2, dh), k_norm_w), cos, sin)
    k_all = jnp.concatenate([k, kc], axis=1)
    v_all = jnp.concatenate([v.reshape(B, S, H, ATTN_V_DIM), vc], axis=1)
    attn = _diff_attn_blocked(q, k_all, v_all, lam)
    y = jnp.concatenate([_attn_post(attn, subln_w, lam_init),
                         _gated_conv(cb, cc, cx, conv_w),
                         _multiscale_pool(pu, pool_w, pool_scale)], axis=-1) @ w_out
    if not ctx_out:
        return y, None
    qc = _rms(qc.reshape(B, Lc, H, 2, dh), q_norm_w)
    attn_c = _diff_attn(qc, kc, vc, lam)
    yc = jnp.concatenate([_attn_post(attn_c, subln_w, lam_init),
                          _gated_conv(cbc, ccc, cxc, conv_w),
                          _multiscale_pool(puc, pool_w, pool_scale)], axis=-1) @ w_out
    return y, yc

def setup_inputs(seed: int = 0) -> dict:
    key = jax.random.key(seed)
    ks = jax.random.split(key, 20)

    def n(k, shape, s):
        return jax.random.normal(k, shape, jnp.float32) * s

    return {
        "x": n(ks[0], (BATCH, SEQ, D_MODEL), 1.0),
        "c": n(ks[1], (BATCH, D_MODEL), 1.0),
        "ctx": n(ks[2], (BATCH, CTX_LEN, D_MODEL), 1.0),
        "c_ctx": n(ks[3], (D_MODEL,), 1.0),
        "norm_w": 1.0 + n(ks[4], (DEPTH, 3, D_MODEL), 0.1),
        "w_mod": n(ks[5], (DEPTH, D_MODEL, N_MOD * D_MODEL), 0.5 * D_MODEL ** -0.5),
        "b_mod": n(ks[6], (DEPTH, N_MOD * D_MODEL), 0.02),
        "ffn1_w_gu": n(ks[7], (DEPTH, D_MODEL, 2 * D_FF), D_MODEL ** -0.5),
        "ffn1_w_down": n(ks[8], (DEPTH, D_FF, D_MODEL), D_FF ** -0.5),
        "ffn2_w_gu": n(ks[9], (DEPTH, D_MODEL, 2 * D_FF), D_MODEL ** -0.5),
        "ffn2_w_down": n(ks[10], (DEPTH, D_FF, D_MODEL), D_FF ** -0.5),
        "w_in": n(ks[11], (DEPTH, D_MODEL, IN_COLS), D_MODEL ** -0.5),
        "w_out": n(ks[12], (DEPTH, MIX_WIDTH, D_MODEL), MIX_WIDTH ** -0.5),
        "q_norm_w": 1.0 + n(ks[13], (DEPTH, ATTN_HEAD_DIM), 0.1),
        "k_norm_w": 1.0 + n(ks[14], (DEPTH, ATTN_HEAD_DIM), 0.1),
        "lambda_qk": n(ks[15], (DEPTH, 4, ATTN_HEAD_DIM), 0.1),
        "subln_w": 1.0 + n(ks[16], (DEPTH, ATTN_V_DIM), 0.1),
        "conv_w": n(ks[17], (DEPTH, CONV_K, CONV_WIDTH), CONV_K ** -0.5),
        "pool_w": n(ks[18], (DEPTH, POOL_GROUPS, POOL_GROUP_DIM, POOL_GROUP_DIM), POOL_GROUP_DIM ** -0.5),
        "pool_scale": 1.0 + n(ks[19], (DEPTH, POOL_WIDTH), 0.1),
    }

def reference(x, c, ctx, c_ctx, norm_w, w_mod, b_mod, ffn1_w_gu, ffn1_w_down,
              ffn2_w_gu, ffn2_w_down, w_in, w_out, q_norm_w, k_norm_w, lambda_qk,
              subln_w, conv_w, pool_w, pool_scale):
    B, S, _ = x.shape
    cos, sin = _axial_rope_tables(S)
    silu_c = jax.nn.silu(c)
    silu_cc = jax.nn.silu(c_ctx)[None]
    h, hc = x, ctx
    for l in range(DEPTH):
        ctx_out = l < DEPTH - 1
        lam_init = 0.8 - 0.6 * math.exp(-0.3 * l)
        mod = (silu_c @ w_mod[l] + b_mod[l]).reshape(B, N_MOD, D_MODEL)
        mod_c = (silu_cc @ w_mod[l] + b_mod[l]).reshape(1, N_MOD, D_MODEL)
        m = [mod[:, i] for i in range(N_MOD)]
        mc = [mod_c[:, i] for i in range(N_MOD)]
        h = h + 0.5 * m[2][:, None] * _swiglu(_modulate(_rms(h, norm_w[l, 0]), m[0], m[1]),
                                              ffn1_w_gu[l], ffn1_w_down[l])
        hc = hc + 0.5 * mc[2][:, None] * _swiglu(_modulate(_rms(hc, norm_w[l, 0]), mc[0], mc[1]),
                                                 ffn1_w_gu[l], ffn1_w_down[l])
        lq = lambda_qk[l].astype(jnp.float32)
        lam = jnp.exp(jnp.sum(lq[0] * lq[1])) - jnp.exp(jnp.sum(lq[2] * lq[3])) + lam_init
        u = _modulate(_rms(h, norm_w[l, 1]), m[3], m[4])
        uc = _modulate(_rms(hc, norm_w[l, 1]), mc[3], mc[4])
        y, yc = _hybrid_mixer(u, uc, ctx_out, w_in[l], w_out[l], q_norm_w[l], k_norm_w[l],
                              lam, lam_init, subln_w[l], conv_w[l], pool_w[l], pool_scale[l],
                              cos, sin)
        h = h + m[5][:, None] * y
        h = h + 0.5 * m[8][:, None] * _swiglu(_modulate(_rms(h, norm_w[l, 2]), m[6], m[7]),
                                              ffn2_w_gu[l], ffn2_w_down[l])
        if ctx_out:
            hc = hc + mc[5][:, None] * yc
            hc = hc + 0.5 * mc[8][:, None] * _swiglu(_modulate(_rms(hc, norm_w[l, 2]), mc[6], mc[7]),
                                                     ffn2_w_gu[l], ffn2_w_down[l])
    return h


_drawn_inputs = setup_inputs


def setup_inputs(seed=0):
    import zlib

    import numpy as np

    out = dict(_drawn_inputs(seed))
    spreads = {}
    factors = {'q_norm_w': 5.227, 'k_norm_w': 5.438, 'lambda_qk': 8.0, 'pool_scale': 3.214}
    for name, (base, spread) in spreads.items():
        noise = np.random.default_rng([zlib.crc32(name.encode()), seed]).standard_normal(out[name].shape)
        drawn = base * np.exp(spread * noise) if base else spread * noise
        out[name] = __import__('jax').numpy.asarray(drawn.astype(out[name].dtype))
    for name, factor in factors.items():
        out[name] = (out[name] * factor).astype(out[name].dtype)
    return out
```

```python
import math
from contextlib import ExitStack

import numpy as np
import concourse.bass as bass
from concourse import mybir
from concourse.alu_op_type import AluOpType as ALU

F32, F32R = mybir.dt.float32, mybir.dt.float32r
ACT = mybir.ActivationFunctionType
AX = mybir.AxisListType

P = 128
D = 1024
DC = D // P
S = 256
T = 2 * S
DEPTH = 2
F_FF = 2816
FC = F_FF // P
H = 4
DH = 64
N_MOD = 9
EPS = 1e-6
WINDOWS = (2, 4, 8, 16)
GRID_W = 64
PADW = 8
PW = S + 2 * PADW

TILES = 8
BLK = TILES * P
RAW = 4
SPL = 2
GU = 2 * FC
DN = FC
HALF = DN // 2
VB, QKB, CB, OB = 4, 8, 8, 8
FFN = GU + DN
MIX = VB + QKB + CB + OB
PER_LAYER = 2 * FFN + MIX
NB = DEPTH * PER_LAYER

COLS = {}
_at = 0
for _name, _n in (("c", DC * 2), ("norm_w", DEPTH * 3 * DC * 2), ("b_mod", DEPTH * N_MOD * DC * 2),
                  ("qw", DEPTH), ("kw", DEPTH), ("subln", DEPTH), ("conv", DEPTH * 2 * 3),
                  ("pscale", DEPTH * 2), ("lam", DEPTH * 4 * DH), ("eps", 1), ("one", 2),
                  ("cos", S), ("sin", S), ("rcnt", 2 * S), ("ones", P), ("halves", P),
                  ("ident", P), ("poolw", DEPTH * 2 * P)):
    COLS[_name] = (_at, _n)
    _at += _n
NCOL = _at


def program(nc, wstream, wmod, cols, x_t, out):
    with ExitStack() as ctx:
        def sb(name, shape, dt=F32):
            return ctx.enter_context(nc.sbuf_tensor(name, shape, dt))

        def sem(name):
            return ctx.enter_context(nc.semaphore(name))

        raw = sb("raw", [P, RAW, BLK])
        whi = sb("whi", [P, SPL, TILES, P], F32R)
        wlo = sb("wlo", [P, SPL, TILES, P], F32R)
        h = sb("h", [P, DC, T])
        xh = sb("xh", [P, DC, T], F32R)
        xl = sb("xl", [P, DC, T], F32R)
        wm = sb("wm", [P, 2, D])
        K = sb("K", [P, NCOL])
        cs = sb("cs", [P, DC * 2])
        modc = sb("modc", [P, DEPTH * N_MOD, DC, 2])
        acol = sb("acol", [P, DEPTH * 3, DC, 2])
        gcol = sb("gcol", [P, DEPTH * 3, DC, 2])
        lamc = sb("lamc", [P, DEPTH, 8])
        lamt = sb("lamt", [P, 2, DH])
        shared_a = sb("shared_a", [P, 4 * T])
        macc = shared_a[:, :].rearrange("p (v n) -> p v n", v=2)
        sq = shared_a[:, 0:2 * T].rearrange("p (a t) -> p a t", a=2)
        ssq = shared_a[:, 2 * T:3 * T]
        shared_b = sb("shared_b", [P, 4 * T])
        sil = shared_b[:, 0:2 * T].rearrange("p (a t) -> p a t", a=2)
        af = shared_b[:, 2 * T:4 * T].rearrange("p (a t) -> p a t", a=2)
        lnv = shared_b[:, 0:T]
        rstd = shared_b[:, T:2 * T]
        xt = shared_b[:, 2 * T:4 * T].rearrange("p (a t) -> p a t", a=4)
        hidden = ExitStack()
        ah = hidden.enter_context(nc.sbuf_tensor("ah", [P, FC * T], F32R))
        al = hidden.enter_context(nc.sbuf_tensor("al", [P, FC * T], F32R))
        hidden.close()
        kq = sb("kq", [P, 8, T])
        vt = sb("vt", [P, 4, T])
        cx = sb("cx", [P, 8, T])
        sqk = sb("sqk", [P, 2, T])
        lnk = sb("lnk", [P, T])
        rq = sb("rq", [P, 2, T])
        shf = sb("shf", [P, S])
        rot = sb("rot", [P, S])
        prob = sb("prob", [P, 2, 2, T])
        att = sb("att", [P, 2, T])
        difT = sb("difT", [P, 2, 4, P])
        amax = sb("amax", [P, 2, 2])
        nmax = sb("nmax", [P, 2, 2])
        lsum = sb("lsum", [P, 2, 2])
        linv = sb("linv", [P, 2, 2])
        nlin = sb("nlin", [P, 2, 1])
        of = sb("of", [P, H, T])
        yf = sb("yf", [P, T])
        dif = yf
        pad0 = sb("pad0", [P, 2, PW])
        pad1 = sb("pad1", [P, 2, PW])
        pooled = cx[:, 0:2, :]
        box = cx[:, 2:4, :].rearrange("p c (s t) -> p c s t", t=S)
        cu = sb("cu", [P, 2, 2, S + 2])
        cy = sb("cy", [P, 2, S])
        ps = ctx.enter_context(nc.psum_tensor("ps", [P, 8, T], F32))

        def col(name, i=0, n=1):
            a = COLS[name][0] + i
            assert i + n <= COLS[name][1]
            return K[:, a:a + n]

        cols_in = sem("cols_in")
        x_in = sem("x_in")
        raw_in = [sem(f"raw_in{i}") for i in range(RAW)]
        hi_done = sem("hi_done")
        lo_done = sem("lo_done")
        block_done = sem("block_done")
        wm_in = [sem(f"wm_in{i}") for i in range(2)]
        cs_done = sem("cs_done")
        mod_acc = sem("mod_acc")
        mod_sum = sem("mod_sum")
        mod_col = sem("mod_col")
        h_done = sem("h_done")
        sq_done = sem("sq_done")
        ssq_done = sem("ssq_done")
        stat_done = sem("stat_done")
        ln_done = sem("ln_done")
        rstd_done = sem("rstd_done")
        xt_done = sem("xt_done")
        xh_done = sem("xh_done")
        xl_done = sem("xl_done")
        silu_done = sem("silu_done")
        mul_done = sem("mul_done")
        ah_done = sem("ah_done")
        al_done = sem("al_done")
        evac = sem("evac")
        sqk_done = sem("sqk_done")
        qk_stat = sem("qk_stat")
        lnk_done = sem("lnk_done")
        rq_done = sem("rq_done")
        qk_used = sem("qk_used")
        qk_ready = sem("qk_ready")
        score_done = sem("score_done")
        max_done = sem("max_done")
        exp_done = sem("exp_done")
        dif_done = sem("dif_done")
        tr_done = sem("tr_done")
        difT_done = sem("difT_done")
        pv_done = sem("pv_done")
        of_done = sem("of_done")
        osq_done = sem("osq_done")
        ostat = sem("ostat")
        orstd = sem("orstd")
        y_done = sem("y_done")
        yh_done = sem("yh_done")
        yl_done = sem("yl_done")
        pooled_done = sem("pooled_done")
        pool_mm = sem("pool_mm")
        dve_step = sem("dve_step")
        act_step = sem("act_step")
        lam_red = sem("lam_red")
        lam_exp = sem("lam_exp")
        out_sem = sem("out_sem")

        def width(m):
            return T if m < 5 else S

        def streams(m):
            return width(m) // S

        XT = [2 * DC * m for m in range(7)]

        def xstep(m, d, s):
            return XT[m] + streams(m) * d + s + 1

        def units(l):
            return [(t, hd) for t in range(4 if l == 0 else 2) for hd in range(H)]

        U0 = [0, 4 * H]
        EV = [0, 20]

        def ntile(l):
            return T if l == 0 else S

        Y0 = [0, 8]
        B_win = [PER_LAYER * l + FFN for l in range(DEPTH)]
        lam_init = [0.8 - 0.6 * math.exp(-0.3 * l) for l in range(DEPTH)]

        block = ctx.enter_context(nc.Block())

        @block.sync
        def _(sp):
            sp.dma_start(K[:, :], cols).then_inc(cols_in, 16)
            for n in range(RAW):
                sp.dma_start(raw[:, n, :], wstream[n]).then_inc(raw_in[n], 16)
                if n == 1:
                    sp.dma_start(h[:, :, :], x_t.rearrange("(c p) t -> p c t", p=P)).then_inc(x_in, 16)
            with sp.Fori(1, NB // RAW) as i:
                for s in range(RAW):
                    sp.wait_ge(lo_done, i * RAW + (s + 1 - RAW))
                    sp.dma_start(raw[:, s, :], wstream[bass.ds(i * RAW + s, 1)].rearrange("a p n -> p (a n)"))\
                        .then_inc(raw_in[s], 16)
            for d in range(DC):
                sp.wait_ge(h_done, 5 * DC + d + 1)
                sp.dma_start(out[d * P:(d + 1) * P, :], h[:, d, 0:S]).then_inc(out_sem, 16)
            sp.wait_ge(out_sem, 16 * DC)

        @block.gpsimd
        def _(pool):
            for c in range(2):
                pool.dma_start(wm[:, c, :], wmod[c]).then_inc(wm_in[c], 16)
            with pool.Fori(1, DEPTH * N_MOD * DC // 2) as i:
                for c in range(2):
                    pool.wait_ge(mod_acc, i * 4 + 2 * (c - 1))
                    pool.dma_start(wm[:, c, :], wmod[bass.ds(i * 2 + c, 1)].rearrange("a p n -> p (a n)"))\
                        .then_inc(wm_in[c], 16)

        @block.scalar
        def _(act):
            def split(n, i=0, k=0):
                s = n % RAW
                act.wait_ge(raw_in[s], i * (16 * k) + 16 * (n // RAW + 1))
                if n >= SPL:
                    act.wait_ge(block_done, i * (4 * k) + (n - SPL + 1))
                act.activation(whi[:, n % SPL, :, :].rearrange("p a b -> p (a b)"), raw[:, s, :], ACT.Copy)\
                    .then_inc(hi_done, 1)

            def split_next(n, i=0, k=0):
                if n + SPL < NB:
                    split(n + SPL, i, k)

            def ffn_epilogue(f, j, j0, i, n, w):
                F0 = FC * f
                act.wait_ge(block_done, i * 4 + (n + 1))
                if F0 + j0 >= 2:
                    act.wait_ge(mul_done, i * 2 + (F0 + j - 1))
                act.activation(sil[:, j % 2, 0:w], ps[:, 2 * (j % 2), 0:w], ACT.Silu).then_inc(silu_done, 1)
                act.wait_ge(mul_done, i * 2 + (F0 + j + 1))
                act.activation(ah[:, bass.ds(i * (2 * T) + j * T, w)], af[:, j % 2, 0:w], ACT.Copy)\
                    .then_inc(ah_done, 1)

            def ffn(l, st):
                f = 2 * l + (st == 2)
                n0 = PER_LAYER * l + (0 if st == 0 else FFN + MIX)
                w = width(3 * l + st)
                for first in (True, False):
                    if first:
                        for e in range(4):
                            split_next(n0 + e)
                            if e % 2:
                                ffn_epilogue(f, e // 2, e // 2, 0, n0 + e, w)
                    else:
                        with act.Fori(1, GU // 4) as i:
                            for e in range(4):
                                split_next(n0 + e, i, 1)
                                if e % 2:
                                    ffn_epilogue(f, e // 2, e // 2 + 2, i, n0 + e, w)
                m = 3 * l + st + 1
                for hf in range(2):
                    nd = n0 + GU + HALF * hf
                    split_next(nd)
                    with act.Fori(0, (HALF - 3) // 4) as i:
                        for e in range(4):
                            split_next(nd + 1 + e, i, 1)
                    split_next(nd + HALF - 2)
                    split_next(nd + HALF - 1)
                    if m < 6:
                        for d in range(4 * hf, 4 * hf + 4):
                            square(m, d)
                if m < 6:
                    norm(m)

            def square(m, d):
                w = width(m)
                g = DC * m + d
                if m == 0:
                    if d == 0:
                        act.wait_ge(x_in, 16)
                else:
                    act.wait_ge(h_done, DC * (m - 1) + d + 1)
                if g >= 2:
                    act.wait_ge(ssq_done, g - 1)
                act.activation(sq[:, g % 2, 0:w], h[:, d, 0:w], ACT.Square).then_inc(sq_done, 1)

            def norm(m):
                w = width(m)
                act.wait_ge(stat_done, m + 1)
                act.activation(lnv[:, 0:w], ps[:, 4, 0:w], ACT.Ln, bias=col("eps"), scale=1.0 / D)\
                    .then_inc(ln_done, 1)
                act.wait_ge(ln_done, m + 1)
                act.activation(rstd[:, 0:w], lnv[:, 0:w], ACT.Exp, scale=-0.5).then_inc(rstd_done, 1)
                l, st = divmod(m, 3)
                for d in range(DC):
                    for s in range(streams(m)):
                        g = xstep(m, d, s)
                        act.wait_ge(xt_done, g)
                        act.activation(xh[:, d, s * S:(s + 1) * S], xt[:, (g - 1) % 4, :], ACT.Identity,
                                       bias=modc[:, N_MOD * l + 3 * st, d, s:s + 1]).then_inc(xh_done, 1)

            def mixer(l):
                n0, w = B_win[l], ntile(l)
                for b in range(VB):
                    split_next(n0 + b)
                for c in range(4):
                    act.activation(vt[:, c, :], ps[:, 4 + c, :], ACT.Copy).then_inc(evac, 1)
                for b in range(QKB):
                    n = n0 + VB + b
                    split_next(n)
                    wb = T if b < 4 else w
                    act.wait_ge(block_done, n + 1)
                    act.activation(kq[:, b, 0:wb], ps[:, b % 4, 0:wb], ACT.Copy).then_inc(evac, 1)
                for b in range(CB):
                    n = n0 + VB + QKB + b
                    wb = T if b < 4 else w
                    if 8 * l + b >= 2:
                        act.wait_ge(qk_stat, 8 * l + b - 1)
                    act.wait_ge(evac, EV[l] + 4 + b + 1)
                    act.activation(sqk[:, b % 2, 0:wb], kq[:, b, 0:wb], ACT.Square).then_inc(sqk_done, 1)
                    split_next(n)
                    act.wait_ge(block_done, n + 1)
                    act.activation(cx[:, b, 0:w], ps[:, b % 4, 0:w], ACT.Copy).then_inc(evac, 1)
                    qk = 8 * l + b
                    act.wait_ge(qk_stat, qk + 1)
                    act.activation(lnk[:, 0:wb], ps[:, 4 + b % 4, 0:wb], ACT.Ln, bias=col("eps"), scale=1.0 / DH)\
                        .then_inc(lnk_done, 1)
                    act.wait_ge(lnk_done, qk + 1)
                    if qk >= 2:
                        act.wait_ge(qk_used, qk - 1)
                    act.activation(rq[:, b % 2, 0:wb], lnk[:, 0:wb], ACT.Exp, scale=-0.5).then_inc(rq_done, 1)
                us = units(l)

                def unit_exp(k):
                    t, _ = us[k]
                    u = U0[l] + k
                    a, wk = (0, T) if t < 2 else (S, S)
                    act.wait_ge(max_done, u + 1)
                    if u >= 2:
                        act.wait_ge(dif_done, u - 1)
                    for b in range(2):
                        act.activation(prob[:, u % 2, b, 0:wk], ps[:, 2 * (u % 2) + b, 0:wk], ACT.Exp,
                                       bias=nmax[:, u % 2, b:b + 1], scale=DH ** -0.5,
                                       accum_out=lsum[:, u % 2, b:b + 1]).then_inc(exp_done, 1)

                def unit_copy(k):
                    u = U0[l] + k
                    nk = 4 if us[k][0] < 2 else 2
                    act.wait_ge(tr_done, u + 1)
                    if u >= 2:
                        act.wait_ge(pv_done, u - 1)
                    act.activation(difT[:, u % 2, 0:nk, :], ps[:, 4 + u % 2, 0:nk * P].rearrange("p (a b) -> p a b", b=P),
                                   ACT.Copy).then_inc(difT_done, 1)

                for k in range(len(us) + 1):
                    if k < len(us):
                        unit_exp(k)
                    if k >= 1:
                        unit_copy(k - 1)
                for hd in range(H):
                    g = H * l + hd
                    if g >= 2:
                        act.wait_ge(ostat, g - 1)
                    act.wait_ge(of_done, (4 if l == 0 else 6))
                    act.activation(sqk[:, hd % 2, 0:w], of[:, hd, 0:w], ACT.Square).then_inc(osq_done, 1)
                    act.wait_ge(ostat, g + 1)
                    act.activation(lnk[:, 0:w], ps[:, 4 + hd % 2, 0:w], ACT.Ln, bias=col("eps"), scale=1.0 / P)\
                        .then_inc(act_step, 1)
                    act.wait_ge(act_step, g + 1)
                    if g >= 2:
                        act.wait_ge(y_done, yidx(l, hd) - 1)
                    act.activation(rq[:, hd % 2, 0:w], lnk[:, 0:w], ACT.Exp, scale=-0.5).then_inc(orstd, 1)
                    act.wait_ge(y_done, yidx(l, hd) + 1)
                    act.activation(xh[:, hd, 0:w], yf[:, 0:w], ACT.Copy).then_inc(yh_done, 1)
                for c in range(4, 8):
                    act.wait_ge(y_done, yidx(l, c) + 1)
                    act.activation(xh[:, c, 0:w], yf[:, 0:w], ACT.Copy).then_inc(yh_done, 1)
                for d in range(OB):
                    split_next(n0 + VB + QKB + CB + d)
                    square(3 * l + 2, d)
                norm(3 * l + 2)

            def yidx(l, c):
                return Y0[l] + c

            act.wait_ge(cols_in, 16)
            act.activation(cs[:, :], col("c", 0, DC * 2), ACT.Silu).then_inc(cs_done, 1)
            split(0)
            split(1)
            act.wait_ge(lam_red, 1)
            act.activation(lamc[:, :, 2:4], lamc[:, :, 0:2], ACT.Exp).then_inc(lam_exp, 1)
            for d in range(DC):
                square(0, d)
            norm(0)
            for l in range(DEPTH):
                ffn(l, 0)
                mixer(l)
                ffn(l, 2)

        @block.vector
        def _(dve):
            steps = [0]

            def own(ins):
                steps[0] += 1
                ins.then_inc(dve_step, 1)
                dve.wait_ge(dve_step, steps[0])

            def split(n, i=0, k=0):
                dve.wait_ge(hi_done, i * (4 * k) + (n + 1))
                dve.tensor_tensor(wlo[:, n % SPL, :, :].rearrange("p a b -> p (a b)"), raw[:, n % RAW, :],
                                  whi[:, n % SPL, :, :].rearrange("p a b -> p (a b)").bitcast(F32), ALU.subtract)\
                    .then_inc(lo_done, 1)

            def split_next(n, i=0, k=0):
                if n + SPL < NB:
                    split(n + SPL, i, k)

            def mod_steps(sec, chunks, i=0):
                for c in chunks:
                    dve.wait_ge(wm_in[c % 2], i * (8 * DC) + 8 * DC * sec + 16 * (c // 2 + 1))
                    if c == 0:
                        if sec > 0:
                            dve.wait_ge(mod_sum, i + sec)
                    for v in range(2):
                        sc = cs[:, 2 * c + v:2 * c + v + 1]
                        if c == 0:
                            ins = dve.tensor_scalar(macc[:, v, :], wm[:, c % 2, :], sc, None, ALU.mult)
                        else:
                            dve.wait_ge(mod_acc, i * (2 * DC) + (2 * DC * sec + 2 * c + v - 1))
                            ins = dve.scalar_tensor_tensor(macc[:, v, :], wm[:, c % 2, :], sc, macc[:, v, :],
                                                           ALU.mult, ALU.add)
                        ins.then_inc(mod_acc, 1)

            def mod_columns(sec, i=0):
                dve.wait_ge(mod_sum, i + (sec + 1))
                a = COLS["b_mod"][0] + sec * 2 * DC
                flat = modc[:, :, :, :].rearrange("p a b c -> p (a b c)")
                dve.tensor_tensor(flat[:, bass.ds(i * (2 * DC) + sec * 2 * DC, 2 * DC)], ps[:, 5, 0:2 * DC],
                                  K[:, bass.ds(i * (2 * DC) + a, 2 * DC)], ALU.add).then_inc(mod_col, 1)

            def ffn_epilogue(f, j, i, w):
                F0 = FC * f
                dve.wait_ge(silu_done, i * 2 + (F0 + j + 1))
                dve.tensor_tensor(af[:, j % 2, 0:w], sil[:, j % 2, 0:w], ps[:, 2 * (j % 2) + 1, 0:w], ALU.mult)\
                    .then_inc(mul_done, 1)
                dve.wait_ge(ah_done, i * 2 + (F0 + j + 1))
                dst = bass.ds(i * (2 * T) + j * T, w)
                dve.tensor_tensor(al[:, dst], af[:, j % 2, 0:w], ah[:, dst].bitcast(F32), ALU.subtract)\
                    .then_inc(al_done, 1)

            def gate_columns(m):
                l, st = divmod(m, 3)
                dve.wait_ge(mod_col, N_MOD * l + 3 * st + 3)
                own(dve.tensor_scalar(gcol[:, m, :, :], modc[:, N_MOD * l + 3 * st + 2, :, :],
                                      1.0 if st == 1 else 0.5, None, ALU.mult))

            def update(m, d, bank):
                for s in range(streams(m)):
                    ins = dve.scalar_tensor_tensor(h[:, d, s * S:(s + 1) * S], ps[:, bank, s * S:(s + 1) * S],
                                                   gcol[:, m, d, s:s + 1], h[:, d, s * S:(s + 1) * S],
                                                   ALU.mult, ALU.add)
                ins.then_inc(h_done, 1)

            def add_square(m, d):
                w = width(m)
                g = DC * m + d
                dve.wait_ge(sq_done, g + 1)
                if d == 0:
                    if m > 0:
                        dve.wait_ge(stat_done, m)
                    dve.tensor_copy(ssq[:, 0:w], sq[:, g % 2, 0:w]).then_inc(ssq_done, 1)
                else:
                    dve.wait_ge(ssq_done, g)
                    dve.tensor_tensor(ssq[:, 0:w], ssq[:, 0:w], sq[:, g % 2, 0:w], ALU.add).then_inc(ssq_done, 1)

            def norm(m):
                l, st = divmod(m, 3)
                w = width(m)
                dve.wait_ge(mod_col, N_MOD * l + 3 * st + 2)
                own(dve.scalar_tensor_tensor(
                    acol[:, m, :, :].rearrange("p a b -> p (a b)"),
                    modc[:, N_MOD * l + 3 * st + 1, :, :].rearrange("p a b -> p (a b)"), 1.0,
                    col("norm_w", m * DC * 2, DC * 2), ALU.add, ALU.mult))
                dve.wait_ge(rstd_done, m + 1)

                def low(d, s):
                    g = xstep(m, d, s)
                    dve.wait_ge(xh_done, g)
                    dve.scalar_tensor_tensor(xl[:, d, s * S:(s + 1) * S], xt[:, (g - 1) % 4, :],
                                             modc[:, N_MOD * l + 3 * st, d, s:s + 1],
                                             xh[:, d, s * S:(s + 1) * S].bitcast(F32), ALU.add, ALU.subtract)\
                        .then_inc(xl_done, 1)

                todo = [(d, s) for d in range(DC) for s in range(streams(m))]
                for q, (d, s) in enumerate(todo):
                    g = xstep(m, d, s)
                    if g > 4:
                        dve.wait_ge(xl_done, g - 4)
                    dve.scalar_tensor_tensor(xt[:, (g - 1) % 4, :], h[:, d, s * S:(s + 1) * S],
                                             acol[:, m, d, s:s + 1], rstd[:, s * S:(s + 1) * S],
                                             ALU.mult, ALU.mult).then_inc(xt_done, 1)
                    if q >= 2:
                        low(*todo[q - 2])
                low(*todo[-2])
                low(*todo[-1])

            def ffn(l, st):
                f = 2 * l + (st == 2)
                m = 3 * l + st
                n0 = PER_LAYER * l + (0 if st == 0 else FFN + MIX)
                w = width(m)
                sec0, nsec = {0: (2, N_MOD - 2), 1: (N_MOD, N_MOD)}.get(f, (0, 0))

                def body(i, sec):
                    for e in range(4):
                        split_next(n0 + e, i, 1)
                        if sec is not None:
                            mod_steps(sec, (2 * e, 2 * e + 1), i)
                        if e % 2:
                            ffn_epilogue(f, e // 2, i, w)
                    if sec is not None:
                        mod_columns(sec, i)

                if nsec:
                    with dve.Fori(0, nsec) as i:
                        body(i, sec0)
                with dve.Fori(nsec, GU // 4) as i:
                    body(i, None)
                gate_columns(m)
                for hf in range(2):
                    nd = n0 + GU + HALF * hf
                    split_next(nd)
                    with dve.Fori(0, (HALF - 3) // 4) as i:
                        for e in range(4):
                            split_next(nd + 1 + e, i, 1)
                    split_next(nd + HALF - 2)
                    split_next(nd + HALF - 1)
                    dve.wait_ge(block_done, nd + HALF)
                    for d in range(4 * hf, 4 * hf + 4):
                        update(m, d, (4 if hf == 0 else 0) + d % 4)
                        if m + 1 < 6 and d > 4 * hf:
                            add_square(m + 1, d - 1)
                    if m + 1 < 6:
                        add_square(m + 1, 4 * hf + 3)
                if m + 1 < 6:
                    norm(m + 1)

            def conv_and_pool(l):
                w = ntile(l)
                ns = w // S
                sv = lambda ap: ap.rearrange("p (s t) -> p s t", t=S)
                dve.memset(pad0[:, :, :], 0.0)
                dve.memset(pad1[:, :, :], 0.0)
                own(dve.memset(cu[:, :, :, :], 0.0))
                dve.wait_ge(evac, EV[l] + 20)
                for c in range(2):
                    for q in range(ns):
                        last = dve.tensor_tensor(cu[:, c, q, 1:S + 1], cx[:, c, q * S:(q + 1) * S],
                                                 cx[:, 2 + c, q * S:(q + 1) * S], ALU.mult)
                for c in range(2):
                    u = cx[:, 6 + c, 0:w]
                    if c == 1:
                        own(last)
                    last = dve.tensor_copy(pad0[:, 0:ns, PADW:PADW + S], sv(u))
                    own(last)
                    src, dst = pad0, pad1
                    for k, win in enumerate(WINDOWS[:2 * c + 2]):
                        half = win // 4
                        lo, hi = {2: (1, PW), 4: (2, PW - 1), 8: (4, PW - 3), 16: (8, PW - 7)}[win]
                        a, b = (1, 0) if k == 0 else (half, -half)
                        own(dve.tensor_tensor(dst[:, 0:ns, lo:hi], src[:, 0:ns, lo - a:hi - a],
                                              src[:, 0:ns, lo - b:hi - b], ALU.add))
                        if k >= 2 * c:
                            g = k - 2 * c
                            pr = slice(64 * g, 64 * g + 64)
                            last = dve.tensor_tensor(box[pr, c, 0:ns, :], dst[pr, 0:ns, PADW:PADW + S],
                                                     rc(c, ns)[pr], ALU.mult)
                        src, dst = dst, src
                    own(last)
                    own(dve.memset(pad0[:, :, :], 0.0))
                    last = dve.tensor_tensor(sv(pooled[:, c, 0:w]), box[:, c, 0:ns, :], sv(u), ALU.subtract)
                    last.then_inc(pooled_done, 1)
                    last = dve.memset(pad1[:, :, :], 0.0)
                own(last)

            def rc(c, ns):
                a = COLS["rcnt"][0] + c * S
                return K[:, a:a + S].rearrange("p (o t) -> p o t", o=1).broadcast_to([P, ns, S])

            def put_y(l, c, ins):
                w = ntile(l)
                ins.then_inc(y_done, 1)
                dve.wait_ge(yh_done, Y0[l] + c + 1)
                dve.tensor_tensor(xl[:, c, 0:w], yf[:, 0:w], xh[:, c, 0:w].bitcast(F32), ALU.subtract)\
                    .then_inc(yl_done, 1)
                dve.wait_ge(yl_done, Y0[l] + c + 1)

            def mixer(l):
                n0, w = B_win[l], ntile(l)
                ns = w // S
                for b in range(VB + QKB):
                    split_next(n0 + b)
                for b in range(CB):
                    split_next(n0 + VB + QKB + b)
                    qk = 8 * l + b
                    wb = T if b < 4 else w
                    dve.wait_ge(rq_done, qk + 1)
                    ins = dve.scalar_tensor_tensor(kq[:, b, 0:wb], kq[:, b, 0:wb], col("kw" if b < 4 else "qw", l),
                                                   rq[:, b % 2, 0:wb], ALU.mult, ALU.mult)
                    ins.then_inc(qk_used, 1)
                    dve.wait_ge(qk_used, qk + 1)
                    own(dve.stream_shuffle(shf[:, :], kq[:, b, 0:S], [(p + 16) % 32 for p in range(32)]))
                    own(dve.tensor_tensor(rot[:, :], shf[:, :], col("sin", 0, S), ALU.mult))
                    own(dve.tensor_tensor(kq[:, b, 0:S], kq[:, b, 0:S], col("cos", 0, S), ALU.mult))
                    own(dve.tensor_tensor(kq[:, b, 0:S], kq[:, b, 0:S], rot[:, :], ALU.add))
                    dve.sem_inc(qk_ready, 1)
                us = units(l)

                def unit_max(k):
                    t, _ = us[k]
                    u = U0[l] + k
                    wk = T if t < 2 else S
                    dve.wait_ge(score_done, u + 1)
                    if u >= 2:
                        dve.wait_ge(exp_done, 2 * (u - 1))
                    dve_b = 2 * (u % 2)
                    own(dve.tensor_reduce(amax[:, u % 2, :], ps[:, dve_b:dve_b + 2, 0:wk], AX.X, ALU.max))
                    dve.tensor_scalar(nmax[:, u % 2, :], amax[:, u % 2, :], -DH ** -0.5, None, ALU.mult)\
                        .then_inc(max_done, 1)

                def unit_dif(k):
                    t, _ = us[k]
                    u = U0[l] + k
                    wk = T if t < 2 else S
                    dve.wait_ge(exp_done, 2 * (u + 1))
                    own(dve.reciprocal(linv[:, u % 2, :], lsum[:, u % 2, :]))
                    own(dve.tensor_tensor(nlin[:, u % 2, :], linv[:, u % 2, 1:2], lamc[:, l, 5:6], ALU.mult))
                    if u >= 1:
                        dve.wait_ge(dif_done, u)
                    own(dve.tensor_scalar(dif[:, 0:wk], prob[:, u % 2, 0, 0:wk], linv[:, u % 2, 0:1], None, ALU.mult))
                    if u >= 2:
                        dve.wait_ge(tr_done, u - 1)
                    dve.scalar_tensor_tensor(att[:, u % 2, 0:wk], prob[:, u % 2, 1, 0:wk], nlin[:, u % 2, :],
                                             dif[:, 0:wk], ALU.mult, ALU.add).then_inc(dif_done, 1)

                def tile_out(t):
                    dve.wait_ge(pv_done, U0[l] + H * (t + 1))
                    dve.tensor_copy(of[:, :, t * P:(t + 1) * P],
                                    ps[:, 6 + t % 2, :].rearrange("p (h q) -> p h q", h=H)).then_inc(of_done, 1)

                for k in range(len(us) + 1):
                    if k < len(us):
                        unit_max(k)
                    if k >= 1:
                        unit_dif(k - 1)
                    if k >= 4 and k % H == 2:
                        tile_out(k // H - 1)
                tile_out(len(us) // H - 1)
                for hd in range(H):
                    g = H * l + hd
                    dve.wait_ge(orstd, g + 1)
                    put_y(l, hd, dve.scalar_tensor_tensor(yf[:, 0:w], of[:, hd, 0:w], lamc[:, l, 6:7],
                                                          rq[:, hd % 2, 0:w], ALU.mult, ALU.mult))
                conv_and_pool(l)
                for c in range(2):
                    cw = COLS["conv"][0] + (2 * l + c) * 3
                    u = cu[:, c, 0:ns, :]
                    y = cy[:, 0:ns, :]
                    own(dve.tensor_scalar(y, u[:, :, 1:S + 1], K[:, cw + 1:cw + 2], None, ALU.mult))
                    own(dve.scalar_tensor_tensor(y, u[:, :, 0:S], K[:, cw:cw + 1], y, ALU.mult, ALU.add))
                    own(dve.scalar_tensor_tensor(y, u[:, :, 2:S + 2], K[:, cw + 2:cw + 3], y, ALU.mult, ALU.add))
                    put_y(l, 4 + c, dve.tensor_tensor(yf[:, 0:w], cy[:, 0:ns, :].rearrange("p s t -> p (s t)"),
                                                      cx[:, 4 + c, 0:w], ALU.mult))
                for c in range(2):
                    dve.wait_ge(pool_mm, 2 * l + c + 1)
                    put_y(l, 6 + c, dve.tensor_scalar(yf[:, 0:w], ps[:, 6 + c, 0:w], col("pscale", 2 * l + c), None,
                                                      ALU.mult))
                m = 3 * l + 1
                gate_columns(m)
                for d in range(OB):
                    n = n0 + VB + QKB + CB + d
                    split_next(n)
                    dve.wait_ge(block_done, n + 1)
                    update(m, d, d % 4)
                    if d >= 1:
                        add_square(m + 1, d - 1)
                add_square(m + 1, OB - 1)
                norm(m + 1)

            dve.wait_ge(cols_in, 16)
            for l in range(DEPTH):
                for b in range(2):
                    a = l * 4 * DH + 2 * b * DH
                    own(dve.tensor_tensor(lamt[:, b, :], col("lam", a, DH), col("lam", a + DH, DH), ALU.mult))
                    own(dve.tensor_reduce(lamc[:, l, b:b + 1], lamt[:, b, :], AX.X, ALU.add))
            dve.sem_inc(lam_red, 1)
            split(0)
            split(1)
            dve.wait_ge(lam_exp, 1)
            for l in range(DEPTH):
                own(dve.tensor_tensor(lamc[:, l, 4:5], lamc[:, l, 3:4], lamc[:, l, 2:3], ALU.subtract))
                own(dve.tensor_scalar(lamc[:, l, 5:6], lamc[:, l, 4:5], lam_init[l], None, ALU.subtract))
                own(dve.tensor_scalar(lamc[:, l, 6:7], col("subln", l), 1.0 - lam_init[l], None, ALU.mult))
            for d in range(DC):
                add_square(0, d)
            dve.wait_ge(cs_done, 1)
            dve.wait_ge(stat_done, 1)
            for sec in range(2):
                mod_steps(sec, range(DC))
                mod_columns(sec)
            norm(0)
            for l in range(DEPTH):
                ffn(l, 0)
                mixer(l)
                ffn(l, 2)

        @block.tensor
        def _(pe):
            def three(out_ap, hi_w, lo_w, hi_x, lo_x, start, stop):
                pe.matmul(out_ap, hi_w, hi_x, start=start, stop=False)
                pe.matmul(out_ap, hi_w, lo_x, start=False, stop=False)
                return pe.matmul(out_ap, lo_w, hi_x, start=False, stop=stop)

            def column_block(n, bank, w, i=0, k=0):
                pe.wait_ge(lo_done, i * (4 * k) + (n + 1))
                for c in range(DC):
                    ins = three(ps[:, bank, 0:w], whi[:, n % SPL, c, :], wlo[:, n % SPL, c, :],
                                xh[:, c, 0:w], xl[:, c, 0:w], c == 0, c == DC - 1)
                ins.then_inc(block_done, 1)

            def mod_sums(sec, i=0):
                pe.wait_ge(mod_acc, i * (2 * DC) + 2 * DC * (sec + 1))
                if sec > 0:
                    pe.wait_ge(mod_col, i + sec)
                for c in range(DC):
                    for v in range(2):
                        ins = pe.matmul(ps[:, 5, 2 * c + v:2 * c + v + 1], macc[:, v, c * P:(c + 1) * P],
                                        col("one", 0, 1), start=True, stop=True)
                ins.then_inc(mod_sum, 1)

            def norm_stat(m):
                w = width(m)
                pe.wait_ge(ssq_done, DC * (m + 1))
                pe.matmul(ps[:, 4, 0:w], col("ones", 0, P), ssq[:, 0:w], start=True, stop=True).then_inc(stat_done, 1)

            def ffn(l, st):
                f = 2 * l + (st == 2)
                m = 3 * l + st
                n0 = PER_LAYER * l + (0 if st == 0 else FFN + MIX)
                w = width(m)
                sec0, nsec = {0: (2, N_MOD - 2), 1: (N_MOD, N_MOD)}.get(f, (0, 0))
                F0 = FC * f
                pe.wait_ge(xl_done, xstep(m, DC - 1, streams(m) - 1))

                def body(i, sec, first):
                    for e in range(4):
                        if e % 2 == 0 and not first:
                            pe.wait_ge(mul_done, i * 2 + (F0 + e // 2 - 1))
                        column_block(n0 + e, e, w, i, 1)
                    if sec is not None:
                        mod_sums(sec, i)

                body(0, sec0 if nsec else None, True)
                if nsec:
                    with pe.Fori(1, nsec) as i:
                        body(i, sec0, False)
                with pe.Fori(max(nsec, 1), GU // 4) as i:
                    body(i, None, False)
                for hf in range(2):
                    nd = n0 + GU + HALF * hf
                    b0 = 4 if hf == 0 else 0

                    def down(b, i=0, k=0):
                        n = nd + b
                        pe.wait_ge(lo_done, i * (4 * k) + (n + 1))
                        if hf == 0:
                            pe.wait_ge(al_done, i * (8 * k) + (F0 + 2 * b + 2))
                        for r in range(2):
                            src = bass.ds(i * (8 * T * k) + (2 * b + r) * T, w)
                            for d in range(4):
                                ins = three(ps[:, b0 + d, 0:w], whi[:, n % SPL, 4 * r + d, :],
                                            wlo[:, n % SPL, 4 * r + d, :], ah[:, src], al[:, src],
                                            b == 0 and r == 0, b == HALF - 1 and r == 1)
                        ins.then_inc(block_done, 1)

                    if hf == 0 and sec0:
                        pe.wait_ge(mod_col, sec0 + nsec)
                    down(0)
                    with pe.Fori(0, (HALF - 3) // 4) as i:
                        for e in range(4):
                            down(1 + e, i, 1)
                    down(HALF - 2)
                    down(HALF - 1)
                if m + 1 < 6:
                    norm_stat(m + 1)

            def mixer(l):
                n0, w = B_win[l], ntile(l)
                m = 3 * l + 1
                pe.wait_ge(xl_done, xstep(m, DC - 1, streams(m) - 1))
                for b in range(VB):
                    n = n0 + b
                    pe.wait_ge(lo_done, n + 1)
                    for r in range(2):
                        c = 2 * b + r
                        wh = whi[:, n % SPL, 4 * r:4 * r + 4, :].rearrange("p a b -> p (a b)")
                        wl = wlo[:, n % SPL, 4 * r:4 * r + 4, :].rearrange("p a b -> p (a b)")
                        for t in range(4):
                            ins = three(ps[:, 4 + t, :], xh[:, c, t * P:(t + 1) * P], xl[:, c, t * P:(t + 1) * P],
                                        wh, wl, c == 0, c == DC - 1)
                    ins.then_inc(block_done, 1)
                for b in range(QKB):
                    if b >= 4:
                        pe.wait_ge(evac, EV[l] + 4 + b - 3)
                    column_block(n0 + VB + b, b % 4, T if b < 4 else w)
                for b in range(CB):
                    pe.wait_ge(evac, EV[l] + 4 + 4 + b + 1)
                    column_block(n0 + VB + QKB + b, b % 4, w)
                    qk, wb = 8 * l + b, T if b < 4 else w
                    pe.wait_ge(sqk_done, qk + 1)
                    if b >= 4:
                        pe.wait_ge(rq_done, qk - 3)
                    pe.matmul(ps[:, 4 + b % 4, 0:wb], col("halves", 0, P), sqk[:, b % 2, 0:wb], start=True, stop=True)\
                        .then_inc(qk_stat, 1)
                us = units(l)
                pe.wait_ge(qk_ready, 8 * (l + 1))
                pe.wait_ge(evac, EV[l] + 20)

                def scores(k):
                    t, hd = us[k]
                    u = U0[l] + k
                    a, wk = (0, T) if t < 2 else (S, S)
                    if k >= 2:
                        pe.wait_ge(exp_done, 2 * (u - 1))
                    for b in range(2):
                        pr = slice(64 * b, 64 * b + 64)
                        ins = pe.matmul(ps[:, 2 * (u % 2) + b, 0:wk], kq[pr, 4 + hd, t * P:(t + 1) * P],
                                        kq[pr, hd, a:a + wk], start=True, stop=True)
                    ins.then_inc(score_done, 1)

                def turn(k):
                    u = U0[l] + k
                    nk = 4 if us[k][0] < 2 else 2
                    pe.wait_ge(dif_done, u + 1)
                    if k >= 2:
                        pe.wait_ge(difT_done, u - 1)
                    for j in range(nk):
                        ins = pe.transpose(ps[:, 4 + u % 2, j * P:(j + 1) * P], att[:, u % 2, j * P:(j + 1) * P],
                                           col("ident", 0, P))
                    ins.then_inc(tr_done, 1)

                def values(k):
                    t, hd = us[k]
                    u = U0[l] + k
                    k0, nk = (0, 4) if t < 2 else (2, 2)
                    pe.wait_ge(difT_done, u + 1)
                    if hd == 0 and t >= 2:
                        pe.wait_ge(of_done, t - 1)
                    for j in range(nk):
                        ins = pe.matmul(ps[:, 6 + t % 2, hd * P:(hd + 1) * P], vt[:, k0 + j, hd * P:(hd + 1) * P],
                                        difT[:, u % 2, j, :], start=(j == 0), stop=(j == nk - 1))
                    ins.then_inc(pv_done, 1)

                for k in range(len(us) + 2):
                    if k < len(us):
                        scores(k)
                    if 1 <= k <= len(us):
                        turn(k - 1)
                    if k >= 2:
                        values(k - 2)
                for hd in range(H):
                    g = H * l + hd
                    pe.wait_ge(osq_done, g + 1)
                    if hd >= 2:
                        pe.wait_ge(orstd, g - 1)
                    pe.matmul(ps[:, 4 + hd % 2, 0:w], col("ones", 0, P), sqk[:, hd % 2, 0:w], start=True, stop=True)\
                        .then_inc(ostat, 1)
                for c in range(2):
                    pe.wait_ge(pooled_done, 2 * l + c + 1)
                    pe.matmul(ps[:, 6 + c, 0:w], col("poolw", (2 * l + c) * P, P), pooled[:, c, 0:w],
                              start=True, stop=True).then_inc(pool_mm, 1)
                pe.wait_ge(yl_done, Y0[l] + 8)
                for d in range(OB):
                    n = n0 + VB + QKB + CB + d
                    if d >= 4:
                        pe.wait_ge(h_done, DC * (3 * l + 1) + d - 3)
                    column_block(n, d % 4, w)
                norm_stat(3 * l + 2)

            pe.wait_ge(cols_in, 16)
            norm_stat(0)
            for sec in range(2):
                mod_sums(sec)
            for l in range(DEPTH):
                ffn(l, 0)
                mixer(l)
                ffn(l, 2)


def blocks_of(w, rows_per_block, col_chunks):
    k, n = w.shape
    a = w.reshape(k // (rows_per_block * P), rows_per_block, P, n // (col_chunks * P), col_chunks * P)
    a = a.transpose(3, 0, 2, 1, 4)
    return a.reshape(-1, P, BLK)


def kernel(x, c, ctx, c_ctx, norm_w, w_mod, b_mod, ffn1_w_gu, ffn1_w_down, ffn2_w_gu, ffn2_w_down,
           w_in, w_out, q_norm_w, k_norm_w, lambda_qk, subln_w, conv_w, pool_w, pool_scale):
    import concourse.bacc as bacc
    from concourse.bass_utils import run_bass_kernel_spmd

    f = lambda a: np.asarray(a)
    stream = []
    for l in range(DEPTH):
        def ffn_blocks(gu, dn):
            g = blocks_of(f(gu)[l], DC, 1)
            return [np.stack([g[:FC], g[FC:]], 1).reshape(-1, P, BLK), blocks_of(f(dn)[l], 2, 4)]
        stream += ffn_blocks(ffn1_w_gu, ffn1_w_down)
        wi = f(w_in)[l]
        W, C = 4 * P, 2 * P
        q, k, v, cb, cc, cxx, pu = (wi[:, a:b] for a, b in
                                    ((0, W), (W, 2 * W), (2 * W, 3 * W), (3 * W, 3 * W + C),
                                     (3 * W + C, 3 * W + 2 * C), (3 * W + 2 * C, 3 * W + 3 * C),
                                     (3 * W + 3 * C, 3 * W + 4 * C)))
        stream += [blocks_of(v, 2, 4)] + [blocks_of(a, DC, 1) for a in (k, q, cc, cxx, cb, pu)]
        stream += [blocks_of(f(w_out)[l], DC, 1)]
        stream += ffn_blocks(ffn2_w_gu, ffn2_w_down)
    wstream = np.concatenate(stream)
    assert wstream.shape[0] == NB
    wmod = np.ascontiguousarray(f(w_mod).reshape(DEPTH, DC, P, N_MOD, D).transpose(0, 3, 1, 2, 4)
                                .reshape(DEPTH * N_MOD * DC, P, D))

    def two(a):
        a = a.reshape(-1, DC, P).transpose(2, 0, 1)
        return np.repeat(a[..., None], 2, -1).reshape(P, -1)

    nf = DH // 4
    inv = 10000.0 ** (-np.arange(nf, dtype=np.float32) / nf)
    t = np.arange(S)
    ang = np.stack([(t // GRID_W)[:, None] * inv, (t % GRID_W)[:, None] * inv], 1).astype(np.float32)
    cos = np.repeat(np.cos(ang)[:, :, None], 2, 2).reshape(S, DH).T
    sin = np.stack([-np.sin(ang), np.sin(ang)], 2).reshape(S, DH).T
    win = np.repeat(np.array(WINDOWS), DH)[:, None]
    cnt = np.minimum(t + win // 2, S) - np.maximum(t - win // 2, 0)
    pw = np.zeros((DEPTH, 2, P, P), np.float32)
    for g in range(4):
        a = slice(64 * (g % 2), 64 * (g % 2) + 64)
        pw[:, g // 2, a, a] = f(pool_w)[:, g]
    pieces = {
        "c": np.stack([f(c)[0], f(c_ctx)], -1).reshape(DC, P, 2).transpose(1, 0, 2).reshape(P, -1),
        "norm_w": two(f(norm_w)),
        "b_mod": two(f(b_mod)),
        "qw": np.tile(f(q_norm_w).T, (2, 1)),
        "kw": np.tile(f(k_norm_w).T, (2, 1)),
        "subln": f(subln_w).T,
        "conv": f(conv_w).reshape(DEPTH, 3, 2, P).transpose(3, 0, 2, 1).reshape(P, -1),
        "pscale": f(pool_scale).reshape(DEPTH * 2, P).T,
        "lam": np.broadcast_to(f(lambda_qk).reshape(1, -1), (P, DEPTH * 4 * DH)),
        "eps": np.full((P, 1), EPS),
        "one": np.ones((P, 2)),
        "cos": np.tile(cos, (2, 1)),
        "sin": np.tile(sin, (2, 1)),
        "rcnt": (1.0 / cnt).reshape(2, P, S).transpose(1, 0, 2).reshape(P, -1),
        "ones": np.ones((P, P)),
        "halves": np.kron(np.eye(2), np.ones((DH, DH))),
        "ident": np.eye(P),
        "poolw": pw.transpose(2, 0, 1, 3).reshape(P, -1),
    }
    cols = np.zeros((P, NCOL), np.float32)
    for name, (a, n) in COLS.items():
        cols[:, a:a + n] = pieces[name]
    x_t = np.ascontiguousarray(np.concatenate([f(x)[0], f(ctx)[0]]).T)

    nc = bacc.Bacc("TRN2", target_bir_lowering=False, num_devices=1)
    arrays = {"wstream": wstream, "wmod": wmod, "cols": cols, "x_t": x_t}
    aps = {n: nc.dram_tensor(n, a.shape, F32, kind="ExternalInput").ap() for n, a in arrays.items()}
    out = nc.dram_tensor("out_t", (D, S), F32, kind="ExternalOutput").ap()
    program(nc, aps["wstream"], aps["wmod"], aps["cols"], aps["x_t"], out)
    r = run_bass_kernel_spmd(nc, [arrays], core_ids=[0])
    return np.ascontiguousarray(r.results[0]["out_t"].T)[None]
```

```python
import math
from contextlib import ExitStack

import numpy as np
import concourse.bass as bass
from concourse import mybir
from concourse.alu_op_type import AluOpType as ALU

F32, F32R = mybir.dt.float32, mybir.dt.float32r
ACT = mybir.ActivationFunctionType
AX = mybir.AxisListType

P = 128
D = 1024
DC = D // P
S = 256
T = 2 * S
DEPTH = 2
F_FF = 2816
FC = F_FF // P
H = 4
DH = 64
N_MOD = 9
EPS = 1e-6
WINDOWS = (2, 4, 8, 16)
GRID_W = 64
PADW = 8
PW = S + 2 * PADW

TILES = 8
BLK = TILES * P
RAW = 4
SPL = 2
GU = 2 * FC
DN = FC
HALF = DN // 2
QKB, CB, VB, OB = 8, 8, 4, 8
CV = QKB + CB
FFN = GU + DN
MIX = VB + QKB + CB + OB
PER_LAYER = 2 * FFN + MIX
NB = DEPTH * PER_LAYER

HN = D // 2
PAIRS = DC // 2
UNITS = DEPTH * N_MOD * 2
UC = HN // P * 2
START_UNITS = 4
UNIT_AT = {0: (4, GU // 4), 1: (16, GU // 4), 2: (27, 9)}
MIX_UNIT = 15

COLS = {}
_at = 0
for _name, _n in (("c", DC * 2), ("norm_w", DEPTH * 3 * DC * 2), ("b_mod", DEPTH * N_MOD * DC * 2),
                  ("eps", 1), ("one", 1), ("sel", 8), ("ones", P),
                  ("qw", DEPTH), ("kw", DEPTH), ("subln", DEPTH), ("conv", DEPTH * 2 * 3),
                  ("pscale", DEPTH * 2), ("lam", DEPTH * 4 * DH),
                  ("cos", S), ("sin", S), ("rcnt", 2 * S), ("halves", P),
                  ("ident", P), ("poolw", DEPTH * 2 * P)):
    COLS[_name] = (_at, _n)
    _at += _n
NCOL = _at
EARLY = COLS["qw"][0]


def program(nc, wstream, wmod, cols, x_t, out):
    with ExitStack() as ctx:
        def sb(name, shape, dt=F32):
            return ctx.enter_context(nc.sbuf_tensor(name, shape, dt))

        def sem(name):
            return ctx.enter_context(nc.semaphore(name))

        raw = sb("raw", [P, RAW, BLK])
        whi = sb("whi", [P, SPL, TILES, P], F32R)
        wlo = sb("wlo", [P, SPL, TILES, P], F32R)
        h = sb("h", [P, DC, T])
        xh = sb("xh", [P, DC, T], F32R)
        xl = sb("xl", [P, DC, T], F32R)
        xh32 = xh[:, :, :].bitcast(F32)
        wm = sb("wm", [P, 2, 2, HN])
        K = sb("K", [P, NCOL])
        cs = sb("cs", [P, DC * 2])
        modc = sb("modc", [P, DEPTH * N_MOD, DC, 2])
        acol = sb("acol", [P, DEPTH * 3, DC, 2])
        gcol = sb("gcol", [P, DEPTH * 3, DC, 2])
        lamc = sb("lamc", [P, DEPTH, 8])
        lamt = sb("lamt", [P, 2, DH])
        shared_a = sb("shared_a", [P, 3 * T])
        macc = shared_a[:, 0:2 * HN].rearrange("p (v n) -> p v n", v=2)
        sq = shared_a[:, 0:2 * T].rearrange("p (a t) -> p a t", a=2)
        ssq = shared_a[:, 2 * T:3 * T]
        shared_b = sb("shared_b", [P, 4 * T])
        sil = shared_b[:, 0:2 * T].rearrange("p (a t) -> p a t", a=2)
        af = shared_b[:, 2 * T:4 * T].rearrange("p (a t) -> p a t", a=2)
        lnv = shared_b[:, 0:T]
        rstd = shared_b[:, T:2 * T]
        xt = shared_b[:, 2 * T:4 * T].rearrange("p (a t) -> p a t", a=4)
        hidden = ExitStack()
        ah = hidden.enter_context(nc.sbuf_tensor("ah", [P, FC * T], F32R))
        al = hidden.enter_context(nc.sbuf_tensor("al", [P, FC * T], F32R))
        hidden.close()
        wm0_place = ExitStack()
        wm0 = wm0_place.enter_context(nc.sbuf_tensor("wm0", [P, PAIRS, START_UNITS, 2, HN], F32))
        wm0_rows = wm0_place.enter_context(nc.sbuf_tensor("wm0_rows", [P, HN], F32))
        wm0_place.close()
        kq = sb("kq", [P, 8, T])
        vt = sb("vt", [P, 4, T])
        cx = sb("cx", [P, 8, T])
        sqk = sb("sqk", [P, 2, T])
        lnk = sb("lnk", [P, T])
        rq = sb("rq", [P, 2, T])
        shf = sb("shf", [P, S])
        rot = sb("rot", [P, S])
        prob = sb("prob", [P, 2, 2, T])
        att = sb("att", [P, 2, T])
        difT = sb("difT", [P, 2, 4, P])
        amax = sb("amax", [P, 2, 2])
        nmax = sb("nmax", [P, 2, 2])
        lsum = sb("lsum", [P, 2, 2])
        linv = sb("linv", [P, 2, 2])
        nlin = sb("nlin", [P, 2, 1])
        dif = sb("dif", [P, T])
        of = sb("of", [P, 2, H, P])
        yf = sb("yf", [P, H, P])
        pad0 = sb("pad0", [P, 2, PW])
        pad1 = sb("pad1", [P, 2, PW])
        pooled = cx[:, 0:2, :]
        ysrc = (4, 5, 0, 1)
        box = cx[:, 2:4, :].rearrange("p c (s t) -> p c s t", t=S)
        cu = sb("cu", [P, 2, 2, S + 2])
        cy = sb("cy", [P, 2, S])
        ps = ctx.enter_context(nc.psum_tensor("ps", [P, 8, T], F32))

        def col(name, i=0, n=1):
            a = COLS[name][0] + i
            assert i + n <= COLS[name][1]
            return K[:, a:a + n]

        cols_in = sem("cols_in")
        x_in = sem("x_in")
        raw_in = [sem(f"raw_in{i}") for i in range(RAW)]
        hi_done = sem("hi_done")
        lo_done = sem("lo_done")
        block_done = sem("block_done")
        wm_in = [sem(f"wm_in{i}") for i in range(2)]
        cs_done = sem("cs_done")
        cols2_in = sem("cols2_in")
        wm0_in = [sem(f"wm0_in{p}") for p in range(PAIRS)]
        rows_zero = sem("rows_zero")
        rows_done = sem("rows_done")
        rows_out = sem("rows_out")
        wm_used = sem("wm_used")
        mod_acc = sem("mod_acc")
        mod_sum = sem("mod_sum")
        mod_col = sem("mod_col")
        dn_done = sem("dn_done")
        h_done = sem("h_done")
        sq_done = sem("sq_done")
        ssq_done = sem("ssq_done")
        stat_done = sem("stat_done")
        ln_done = sem("ln_done")
        rstd_done = sem("rstd_done")
        xt_done = sem("xt_done")
        xh_done = sem("xh_done")
        xl_done = sem("xl_done")
        silu_done = sem("silu_done")
        mul_done = sem("mul_done")
        ah_done = sem("ah_done")
        al_done = sem("al_done")
        evac = sem("evac")
        sqk_done = sem("sqk_done")
        qk_stat = sem("qk_stat")
        lnk_done = sem("lnk_done")
        rq_done = sem("rq_done")
        qk_used = sem("qk_used")
        qk_ready = sem("qk_ready")
        score_done = sem("score_done")
        max_done = sem("max_done")
        exp_done = sem("exp_done")
        dif_done = sem("dif_done")
        tr_done = sem("tr_done")
        difT_done = sem("difT_done")
        pv_done = sem("pv_done")
        of_done = sem("of_done")
        osq_done = sem("osq_done")
        ostat = sem("ostat")
        orstd = sem("orstd")
        oln = sem("oln")
        y_done = sem("y_done")
        yh_done = sem("yh_done")
        yl_done = sem("yl_done")
        pooled_done = sem("pooled_done")
        pool_mm = sem("pool_mm")
        dve_step = sem("dve_step")
        lam_red = sem("lam_red")
        lam_exp = sem("lam_exp")
        out_sem = sem("out_sem")

        def width(m):
            return T if m < 5 else S

        def streams(m):
            return width(m) // S

        XT = [2 * DC * m for m in range(7)]

        def xstep(m, d, s):
            return XT[m] + DC * s + d + 1

        def units(l):
            return [(t, hd) for t in range(4 if l == 0 else 2) for hd in range(H)]

        U0 = [0, 4 * H]
        EV = [0, 20]

        def ntile(l):
            return T if l == 0 else S

        NT = [4, 2]
        TB = [0, 4]
        Y0 = [0, 8]

        def unit_steps(u):
            return 2 * DC * (u - START_UNITS)
        B_win = [PER_LAYER * l + FFN for l in range(DEPTH)]
        lam_init = [0.8 - 0.6 * math.exp(-0.3 * l) for l in range(DEPTH)]

        block = ctx.enter_context(nc.Block())

        @block.sync
        def _(sp):
            sp.dma_start(K[:, 0:EARLY], cols[:, 0:EARLY]).then_inc(cols_in, 16)
            sp.dma_start(h[:, :, :], x_t.rearrange("(c p) t -> p c t", p=P)).then_inc(x_in, 16)
            start_pairs = wmod[0:START_UNITS * PAIRS].rearrange("(u q) p n -> q p u n", q=PAIRS)
            for p in range(PAIRS):
                sp.dma_start(wm0[:, p, :, :, :].rearrange("p u a n -> p u (a n)"), start_pairs[p])\
                    .then_inc(wm0_in[p], 16)
            for n in range(RAW):
                sp.dma_start(raw[:, n, :], wstream[n]).then_inc(raw_in[n], 16)
                if n == 1:
                    sp.dma_start(K[:, EARLY:NCOL], cols[:, EARLY:NCOL]).then_inc(cols2_in, 16)
            with sp.Fori(1, NB // RAW) as i:
                for s in range(RAW):
                    sp.wait_ge(lo_done, i * RAW + (s + 1 - RAW))
                    sp.dma_start(raw[:, s, :], wstream[bass.ds(i * RAW + s, 1)].rearrange("a p n -> p (a n)"))\
                        .then_inc(raw_in[s], 16)
            for d in range(DC):
                sp.wait_ge(h_done, 5 * DC + d + 1)
                sp.dma_start(out[d * P:(d + 1) * P, :], h[:, d, 0:S]).then_inc(out_sem, 16)
            sp.wait_ge(out_sem, 16 * DC)

        @block.gpsimd
        def _(pool):
            u0 = START_UNITS * PAIRS
            for c in range(2):
                pool.dma_start(wm[:, c, :, :].rearrange("p a n -> p (a n)"), wmod[u0 + c]).then_inc(wm_in[c], 16)
            with pool.Fori(u0 // 2 + 1, UNITS * PAIRS // 2) as i:
                for c in range(2):
                    pool.wait_ge(wm_used, i * 2 + (c - 1 - u0))
                    pool.dma_start(wm[:, c, :, :].rearrange("p a n -> p (a n)"),
                                   wmod[bass.ds(i * 2 + c, 1)].rearrange("a p n -> p (a n)"))\
                        .then_inc(wm_in[c], 16)

        @block.scalar
        def _(act):
            def split(n, i=0, k=0):
                s = n % RAW
                act.wait_ge(raw_in[s], i * (16 * k) + 16 * (n // RAW + 1))
                if n >= SPL:
                    act.wait_ge(block_done, i * (4 * k) + (n - SPL + 1))
                act.activation(whi[:, n % SPL, :, :].rearrange("p a b -> p (a b)"), raw[:, s, :], ACT.Copy)\
                    .then_inc(hi_done, 1)

            def split_next(n, i=0, k=0):
                if n + SPL < NB:
                    split(n + SPL, i, k)

            def ffn_epilogue(f, j, j0, i, n, w):
                F0 = FC * f
                act.wait_ge(block_done, i * 4 + (n + 1))
                if F0 + j0 >= 2:
                    act.wait_ge(mul_done, i * 2 + (F0 + j - 1))
                act.activation(sil[:, j % 2, 0:w], ps[:, 2 * (j % 2), 0:w], ACT.Silu).then_inc(silu_done, 1)
                act.wait_ge(mul_done, i * 2 + (F0 + j + 1))
                act.activation(ah[:, bass.ds(i * (2 * T) + j * T, w)], af[:, j % 2, 0:w], ACT.Copy)\
                    .then_inc(ah_done, 1)

            def ffn(l, st):
                f = 2 * l + (st == 2)
                n0 = PER_LAYER * l + (0 if st == 0 else FFN + MIX)
                w = width(3 * l + st)
                for first in (True, False):
                    if first:
                        for e in range(4):
                            split_next(n0 + e)
                            if e % 2:
                                ffn_epilogue(f, e // 2, e // 2, 0, n0 + e, w)
                    else:
                        with act.Fori(1, GU // 4) as i:
                            for e in range(4):
                                split_next(n0 + e, i, 1)
                                if e % 2:
                                    ffn_epilogue(f, e // 2, e // 2 + 2, i, n0 + e, w)
                m = 3 * l + st + 1
                for hf in range(2):
                    nd = n0 + GU + HALF * hf
                    split_next(nd)
                    with act.Fori(0, (HALF - 3) // 4) as i:
                        for e in range(4):
                            split_next(nd + 1 + e, i, 1)
                    split_next(nd + HALF - 2)
                    if hf == 0:
                        split_next(nd + HALF - 1)
                    if m < 6:
                        if hf == 1:
                            ln_exp_tables()
                        for d in range(4 * hf, 4 * hf + 4):
                            square(m, d)
                    if hf == 1:
                        split_next(nd + HALF - 1)
                if m < 6:
                    norm(m)

            def ln_exp_tables():
                act.preload_act_table_set("natural_log_exp_and_others")

            def square(m, d):
                w = width(m)
                g = DC * m + d
                if m == 0:
                    if d == 0:
                        act.wait_ge(x_in, 16)
                else:
                    act.wait_ge(h_done, DC * (m - 1) + d + 1)
                if d >= 2:
                    act.wait_ge(ssq_done, (DC - 1) * m + d - 1)
                elif m > 0:
                    act.wait_ge(stat_done, m)
                act.activation(sq[:, g % 2, 0:w], h[:, d, 0:w], ACT.Square).then_inc(sq_done, 1)

            def norm(m):
                w = width(m)
                act.wait_ge(stat_done, m + 1)
                act.activation(lnv[:, 0:w], ps[:, 4, 0:w], ACT.Ln, bias=col("eps"), scale=1.0 / D)\
                    .then_inc(ln_done, 1)
                act.wait_ge(ln_done, m + 1)
                act.activation(rstd[:, 0:w], lnv[:, 0:w], ACT.Exp, scale=-0.5).then_inc(rstd_done, 1)
                l, st = divmod(m, 3)
                for s in range(streams(m)):
                    for d in range(DC):
                        g = xstep(m, d, s)
                        act.wait_ge(xt_done, g)
                        act.activation(xh[:, d, s * S:(s + 1) * S], xt[:, (g - 1) % 4, :], ACT.Identity,
                                       bias=modc[:, N_MOD * l + 3 * st, d, s:s + 1]).then_inc(xh_done, 1)

            def mixer(l):
                n0, w = B_win[l], ntile(l)

                def wid(b):
                    return T if b < 4 else w

                for b in range(QKB + CB):
                    split_next(n0 + b)
                    act.wait_ge(block_done, n0 + b + 1)
                    dst = kq[:, b, 0:wid(b)] if b < QKB else cx[:, b - QKB, 0:w]
                    act.activation(dst, ps[:, b % 4, 0:wid(b)], ACT.Copy).then_inc(evac, 1)
                    if b < QKB:
                        if b >= 2:
                            act.wait_ge(qk_stat, 8 * l + b - 1)
                        act.activation(sqk[:, b % 2, 0:wid(b)], ps[:, b % 4, 0:wid(b)], ACT.Square)\
                            .then_inc(sqk_done, 1)
                    if 1 <= b <= QKB:
                        qk, c = 8 * l + b - 1, b - 1
                        act.wait_ge(qk_stat, qk + 1)
                        if qk >= 1:
                            act.wait_ge(rq_done, qk)
                        act.activation(lnk[:, 0:wid(c)], ps[:, 6 + c % 2, 0:wid(c)], ACT.Ln, bias=col("eps"),
                                       scale=1.0 / DH).then_inc(lnk_done, 1)
                        act.wait_ge(lnk_done, qk + 1)
                        if c >= 2:
                            act.wait_ge(qk_used, qk - 1)
                        act.activation(rq[:, c % 2, 0:wid(c)], lnk[:, 0:wid(c)], ACT.Exp, scale=-0.5)\
                            .then_inc(rq_done, 1)
                for b in range(VB):
                    split_next(n0 + CV + b)
                act.wait_ge(block_done, n0 + CV + VB)
                for c in range(4):
                    act.activation(vt[:, c, :], ps[:, 4 + c, :], ACT.Copy).then_inc(evac, 1)
                us = units(l)

                def unit_exp(k):
                    t, _ = us[k]
                    u = U0[l] + k
                    a, wk = (0, T) if t < 2 else (S, S)
                    act.wait_ge(max_done, u + 1)
                    if u >= 2:
                        act.wait_ge(dif_done, u - 1)
                    for b in range(2):
                        act.activation(prob[:, u % 2, b, 0:wk], ps[:, 2 * (u % 2) + b, 0:wk], ACT.Exp,
                                       bias=nmax[:, u % 2, b:b + 1], scale=DH ** -0.5,
                                       accum_out=lsum[:, u % 2, b:b + 1]).then_inc(exp_done, 1)

                def unit_copy(k):
                    u = U0[l] + k
                    nk = 4 if us[k][0] < 2 else 2
                    act.wait_ge(tr_done, u + 1)
                    if u >= 2:
                        act.wait_ge(pv_done, u - 1)
                    act.activation(difT[:, u % 2, 0:nk, :], ps[:, 4 + u % 2, 0:nk * P].rearrange("p (a b) -> p a b", b=P),
                                   ACT.Copy).then_inc(difT_done, 1)

                def tile_square(t):
                    g = TB[l] + t
                    act.wait_ge(of_done, g + 1)
                    act.activation(sqk[:, g % 2, :], of[:, g % 2, :, :].rearrange("p h q -> p (h q)"), ACT.Square)\
                        .then_inc(osq_done, 1)

                def tile_rstd(t):
                    g = TB[l] + t
                    act.wait_ge(ostat, g + 1)
                    if t >= 1:
                        act.wait_ge(orstd, g)
                    else:
                        act.wait_ge(rq_done, 8 * (l + 1))
                    act.activation(lnk[:, :], ps[:, 6 + t % 2, :], ACT.Ln, bias=col("eps"), scale=1.0 / P)\
                        .then_inc(oln, 1)
                    act.wait_ge(oln, g + 1)
                    act.activation(rq[:, g % 2, :], lnk[:, :], ACT.Exp, scale=-0.5).then_inc(orstd, 1)

                def tile_high(t):
                    act.wait_ge(y_done, Y0[l] + 4 + t + 1)
                    act.activation(xh[:, 0:H, t * P:(t + 1) * P], yf[:, :, :], ACT.Copy).then_inc(yh_done, 1)

                for k in range(len(us) + 6):
                    if k < len(us):
                        unit_exp(k)
                    if 2 <= k <= len(us) + 1:
                        unit_copy(k - 2)
                    if k < 4:
                        act.wait_ge(y_done, Y0[l] + k + 1)
                        act.activation(xh[:, 4 + k, 0:w], cx[:, ysrc[k], 0:w], ACT.Copy).then_inc(yh_done, 1)
                    if k >= 7 and (k - 7) % H == 0 and (k - 7) // H < NT[l]:
                        tile_square((k - 7) // H)
                    if k >= 8 and (k - 8) % H == 0 and (k - 8) // H < NT[l]:
                        tile_rstd((k - 8) // H)
                    if k >= 9 and (k - 9) % H == 0 and (k - 9) // H < NT[l]:
                        tile_high((k - 9) // H)
                for d in range(OB):
                    if d < OB - 1:
                        split_next(n0 + CV + VB + d)
                    square(3 * l + 2, d)
                split_next(n0 + CV + VB + OB - 1)
                norm(3 * l + 2)

            act.wait_ge(cols_in, 16)
            act.activation(cs[:, :], col("c", 0, DC * 2), ACT.Silu).then_inc(cs_done, 1)
            ln_exp_tables()
            for d in range(DC):
                square(0, d)
            split(0)
            split(1)
            norm(0)
            act.wait_ge(lam_red, 1)
            act.activation(lamc[:, :, 2:4], lamc[:, :, 0:2], ACT.Exp).then_inc(lam_exp, 1)
            for l in range(DEPTH):
                ffn(l, 0)
                mixer(l)
                ffn(l, 2)

        @block.vector
        def _(dve):
            steps = [0]

            def own(ins):
                steps[0] += 1
                ins.then_inc(dve_step, 1)
                dve.wait_ge(dve_step, steps[0])

            def split(n, i=0, k=0):
                dve.wait_ge(hi_done, i * (4 * k) + (n + 1))
                dve.tensor_tensor(wlo[:, n % SPL, :, :].rearrange("p a b -> p (a b)"), raw[:, n % RAW, :],
                                  whi[:, n % SPL, :, :].rearrange("p a b -> p (a b)").bitcast(F32), ALU.subtract)\
                    .then_inc(lo_done, 1)

            def split_next(n, i=0, k=0):
                if n + SPL < NB:
                    split(n + SPL, i, k)

            def mod_pair(u, p, i=0):
                base = unit_steps(u)
                dve.wait_ge(wm_in[p % 2], i * (16 * PAIRS // 2) + 16 * (((u - START_UNITS) * PAIRS + p) // 2 + 1))
                for r in range(2):
                    c = 2 * p + r
                    for v in range(2):
                        sc = cs[:, 2 * c + v:2 * c + v + 1]
                        src, acc = wm[:, p % 2, r, :], macc[:, v, :]
                        if c == 0:
                            ins = dve.tensor_scalar(acc, src, sc, None, ALU.mult)
                        else:
                            dve.wait_ge(mod_acc, i * (2 * DC) + (base + 2 * c + v - 1))
                            ins = dve.scalar_tensor_tensor(acc, src, sc, acc, ALU.mult, ALU.add)
                        ins.then_inc(mod_acc, 1)
                dve.wait_ge(mod_acc, i * (2 * DC) + (base + 4 * p + 4))
                dve.sem_inc(wm_used, 1)

            def mod_columns(u, n=1, i=0):
                dve.wait_ge(mod_sum, i + (u + n))
                a = COLS["b_mod"][0] + u * UC
                flat = modc[:, :, :, :].rearrange("p a b c -> p (a b c)")
                dve.tensor_tensor(flat[:, bass.ds(i * UC + u * UC, n * UC)], ps[:, 5, 0:n * UC],
                                  K[:, bass.ds(i * UC + a, n * UC)], ALU.add).then_inc(mod_col, n)

            def ffn_epilogue(f, j, i, w):
                F0 = FC * f
                dve.wait_ge(silu_done, i * 2 + (F0 + j + 1))
                dve.tensor_tensor(af[:, j % 2, 0:w], sil[:, j % 2, 0:w], ps[:, 2 * (j % 2) + 1, 0:w], ALU.mult)\
                    .then_inc(mul_done, 1)
                dve.wait_ge(ah_done, i * 2 + (F0 + j + 1))
                dst = bass.ds(i * (2 * T) + j * T, w)
                dve.tensor_tensor(al[:, dst], af[:, j % 2, 0:w], ah[:, dst].bitcast(F32), ALU.subtract)\
                    .then_inc(al_done, 1)

            def gate_columns(m):
                l, st = divmod(m, 3)
                dve.wait_ge(mod_col, 2 * (N_MOD * l + 3 * st + 3))
                own(dve.tensor_scalar(gcol[:, m, :, :], modc[:, N_MOD * l + 3 * st + 2, :, :],
                                      1.0 if st == 1 else 0.5, None, ALU.mult))

            def update(m, d, bank):
                for s in range(streams(m)):
                    ins = dve.scalar_tensor_tensor(h[:, d, s * S:(s + 1) * S], ps[:, bank, s * S:(s + 1) * S],
                                                   gcol[:, m, d, s:s + 1], h[:, d, s * S:(s + 1) * S],
                                                   ALU.mult, ALU.add)
                ins.then_inc(h_done, 1)

            def add_square(m, d):
                w = width(m)
                g = DC * m + d
                dve.wait_ge(sq_done, g + 1)
                if d == 0:
                    if m > 0:
                        dve.wait_ge(stat_done, m)
                    dve.tensor_copy(ssq[:, 0:w], sq[:, g % 2, 0:w]).then_inc(ssq_done, 1)
                else:
                    dve.wait_ge(ssq_done, (DC - 1) * m + d)
                    dve.tensor_tensor(ssq[:, 0:w], ssq[:, 0:w], sq[:, g % 2, 0:w], ALU.add).then_inc(ssq_done, 1)

            def norm(m):
                l, st = divmod(m, 3)
                w = width(m)
                dve.wait_ge(mod_col, 2 * (N_MOD * l + 3 * st + 2))
                own(dve.scalar_tensor_tensor(
                    acol[:, m, :, :].rearrange("p a b -> p (a b)"),
                    modc[:, N_MOD * l + 3 * st + 1, :, :].rearrange("p a b -> p (a b)"), 1.0,
                    col("norm_w", m * DC * 2, DC * 2), ALU.add, ALU.mult))
                dve.wait_ge(rstd_done, m + 1)

                def low(d, s):
                    g = xstep(m, d, s)
                    dve.wait_ge(xh_done, g)
                    dve.scalar_tensor_tensor(xl[:, d, s * S:(s + 1) * S], xt[:, (g - 1) % 4, :],
                                             modc[:, N_MOD * l + 3 * st, d, s:s + 1],
                                             xh[:, d, s * S:(s + 1) * S].bitcast(F32), ALU.add, ALU.subtract)\
                        .then_inc(xl_done, 1)

                todo = [(d, s) for s in range(streams(m)) for d in range(DC)]
                for q, (d, s) in enumerate(todo):
                    g = xstep(m, d, s)
                    if g > 4:
                        dve.wait_ge(xl_done, g - 4)
                    dve.scalar_tensor_tensor(xt[:, (g - 1) % 4, :], h[:, d, s * S:(s + 1) * S],
                                             acol[:, m, d, s:s + 1], rstd[:, s * S:(s + 1) * S],
                                             ALU.mult, ALU.mult).then_inc(xt_done, 1)
                    if q >= 2:
                        low(*todo[q - 2])
                low(*todo[-2])
                low(*todo[-1])

            def ffn(l, st):
                f = 2 * l + (st == 2)
                m = 3 * l + st
                n0 = PER_LAYER * l + (0 if st == 0 else FFN + MIX)
                w = width(m)
                u0, nu = UNIT_AT.get(f, (0, 0))

                def body(i, unit, columns):
                    for e in range(4):
                        split_next(n0 + e, i, 1)
                        if e == 0 and columns:
                            mod_columns(u0 - 1, 1, i)
                        if unit:
                            mod_pair(u0, e, i)
                        if e % 2:
                            ffn_epilogue(f, e // 2, i, w)

                body(0, nu > 0, False)
                if nu:
                    with dve.Fori(1, nu) as i:
                        body(i, True, True)
                if nu == GU // 4:
                    mod_columns(u0 + nu - 1)
                elif nu:
                    with dve.Fori(nu, nu + 1) as i:
                        body(i, False, True)
                if nu + 1 < GU // 4:
                    with dve.Fori(nu + 1, GU // 4) as i:
                        body(i, False, False)
                gate_columns(m)

                def half_out(hf, ds):
                    for d in ds:
                        if hf == 1 and d < 7:
                            dve.wait_ge(dn_done, 3 * f + d - 3)
                        else:
                            dve.wait_ge(block_done, n0 + GU + HALF * (hf + 1))
                        update(m, d, (4 if hf == 0 else 0) + d % 4)
                        if m + 1 < 6 and d > 4 * hf:
                            add_square(m + 1, d - 1)
                    if m + 1 < 6 and hf == 0:
                        add_square(m + 1, 3)

                for hf in range(2):
                    nd = n0 + GU + HALF * hf
                    split_next(nd)
                    with dve.Fori(0, (HALF - 3) // 4) as i:
                        for e in range(4):
                            split_next(nd + 1 + e, i, 1)
                    split_next(nd + HALF - 2)
                    if hf == 0:
                        split_next(nd + HALF - 1)
                    half_out(hf, range(4 * hf, 4 * hf + 4))
                    if hf == 1:
                        split_next(nd + HALF - 1)
                if m + 1 < 6:
                    norm(m + 1)

            def conv(l, c):
                ns = ntile(l) // S
                sv = lambda j: cx[:, j, 0:ns * S].rearrange("p (s t) -> p s t", t=S)
                if c == 0:
                    own(dve.memset(cu[:, :, :, :], 0.0))
                cw = COLS["conv"][0] + (2 * l + c) * 3
                u = cu[:, c, 0:ns, :]
                y = cy[:, 0:ns, :]
                own(dve.tensor_tensor(u[:, :, 1:S + 1], sv(c), sv(2 + c), ALU.mult))
                own(dve.tensor_scalar(y, u[:, :, 1:S + 1], K[:, cw + 1:cw + 2], None, ALU.mult))
                own(dve.scalar_tensor_tensor(y, u[:, :, 0:S], K[:, cw:cw + 1], y, ALU.mult, ALU.add))
                own(dve.scalar_tensor_tensor(y, u[:, :, 2:S + 2], K[:, cw + 2:cw + 3], y, ALU.mult, ALU.add))
                dve.tensor_tensor(sv(4 + c), y, sv(4 + c), ALU.mult).then_inc(y_done, 1)
                dve.wait_ge(y_done, Y0[l] + c + 1)

            def pool_chunk(l, c):
                ns = ntile(l) // S
                sv = lambda j: cx[:, j, 0:ns * S].rearrange("p (s t) -> p s t", t=S)
                dve.memset(pad0[:, :, :], 0.0)
                own(dve.memset(pad1[:, :, :], 0.0))
                own(dve.tensor_copy(pad0[:, 0:ns, PADW:PADW + S], sv(6 + c)))
                src, dst = pad0, pad1
                for k, win in enumerate(WINDOWS[:2 * c + 2]):
                    a, b = (1, 0) if k == 0 else (win // 4, -(win // 4))
                    lo, hi = win // 2, PW - win // 2 + 1
                    own(dve.tensor_tensor(dst[:, 0:ns, lo:hi], src[:, 0:ns, lo - a:hi - a],
                                          src[:, 0:ns, lo - b:hi - b], ALU.add))
                    if k >= 2 * c:
                        g = k - 2 * c
                        pr = slice(64 * g, 64 * g + 64)
                        own(dve.tensor_tensor(box[pr, c, 0:ns, :], dst[pr, 0:ns, PADW:PADW + S], rc(c, ns)[pr],
                                              ALU.mult))
                    src, dst = dst, src
                dve.tensor_tensor(sv(c), box[:, c, 0:ns, :], sv(6 + c), ALU.subtract).then_inc(pooled_done, 1)

            def rc(c, ns):
                a = COLS["rcnt"][0] + c * S
                return K[:, a:a + S].rearrange("p (o t) -> p o t", o=1).broadcast_to([P, ns, S])

            def rope(l, b):
                qk = 8 * l + b
                wb = T if b < 4 else ntile(l)
                dve.wait_ge(rq_done, qk + 1)
                dve.scalar_tensor_tensor(kq[:, b, 0:wb], kq[:, b, 0:wb], col("kw" if b < 4 else "qw", l),
                                         rq[:, b % 2, 0:wb], ALU.mult, ALU.mult).then_inc(qk_used, 1)
                dve.wait_ge(qk_used, qk + 1)
                own(dve.stream_shuffle(shf[:, :], kq[:, b, 0:S], [(p + 16) % 32 for p in range(32)]))
                dve.tensor_tensor(kq[:, b, 0:S], kq[:, b, 0:S], col("cos", 0, S), ALU.mult)
                own(dve.tensor_tensor(rot[:, :], shf[:, :], col("sin", 0, S), ALU.mult))
                dve.tensor_tensor(kq[:, b, 0:S], kq[:, b, 0:S], rot[:, :], ALU.add).then_inc(qk_ready, 1)

            def mixer(l):
                n0, w = B_win[l], ntile(l)
                for b in range(QKB + CB + VB):
                    split_next(n0 + b)
                    if 1 <= b <= QKB:
                        rope(l, b - 1)
                    if l == 0 and QKB < b <= QKB + PAIRS:
                        mod_pair(MIX_UNIT, b - QKB - 1)
                    if l == 0 and b == QKB + PAIRS + 2:
                        mod_columns(MIX_UNIT)
                    if b in (QKB + 6, QKB + 7):
                        dve.wait_ge(evac, EV[l] + b - 1)
                        conv(l, b - QKB - 6)
                    if b in (CV, CV + 1):
                        dve.wait_ge(evac, EV[l] + 16)
                        pool_chunk(l, b - CV)
                for c in range(2):
                    dve.wait_ge(pool_mm, 2 * l + c + 1)
                    dve.tensor_scalar(cx[:, c, 0:w], ps[:, c, 0:w], col("pscale", 2 * l + c), None, ALU.mult)\
                        .then_inc(y_done, 1)
                us = units(l)

                def unit_max(k):
                    t, _ = us[k]
                    u = U0[l] + k
                    wk = T if t < 2 else S
                    dve.wait_ge(score_done, u + 1)
                    if u >= 2:
                        dve.wait_ge(exp_done, 2 * (u - 1))
                    b0 = 2 * (u % 2)
                    own(dve.tensor_reduce(amax[:, u % 2, :], ps[:, b0:b0 + 2, 0:wk], AX.X, ALU.max))
                    dve.tensor_scalar(nmax[:, u % 2, :], amax[:, u % 2, :], -DH ** -0.5, None, ALU.mult)\
                        .then_inc(max_done, 1)

                def unit_dif(k):
                    t, _ = us[k]
                    u = U0[l] + k
                    wk = T if t < 2 else S
                    dve.wait_ge(exp_done, 2 * (u + 1))
                    own(dve.reciprocal(linv[:, u % 2, :], lsum[:, u % 2, :]))
                    dve.tensor_tensor(nlin[:, u % 2, :], linv[:, u % 2, 1:2], lamc[:, l, 5:6], ALU.mult)
                    own(dve.tensor_scalar(dif[:, 0:wk], prob[:, u % 2, 0, 0:wk], linv[:, u % 2, 0:1], None, ALU.mult))
                    if u >= 2:
                        dve.wait_ge(tr_done, u - 1)
                    dve.scalar_tensor_tensor(att[:, u % 2, 0:wk], prob[:, u % 2, 1, 0:wk], nlin[:, u % 2, :],
                                             dif[:, 0:wk], ALU.mult, ALU.add).then_inc(dif_done, 1)
                    dve.wait_ge(dif_done, u + 1)

                def tile_out(t):
                    g = TB[l] + t
                    dve.wait_ge(pv_done, U0[l] + H * (t + 1))
                    dve.tensor_copy(of[:, g % 2, :, :], ps[:, 6 + t % 2, :].rearrange("p (h q) -> p h q", h=H))\
                        .then_inc(of_done, 1)

                def tile_scale(t):
                    g = TB[l] + t
                    dve.wait_ge(orstd, g + 1)
                    flat = lambda a: a.rearrange("p h q -> p (h q)")
                    dve.scalar_tensor_tensor(flat(yf[:, :, :]), flat(of[:, g % 2, :, :]), lamc[:, l, 6:7],
                                             rq[:, g % 2, :], ALU.mult, ALU.mult).then_inc(y_done, 1)

                def tile_low(t):
                    dve.wait_ge(yh_done, Y0[l] + 4 + t + 1)
                    q = slice(t * P, (t + 1) * P)
                    dve.tensor_tensor(xl[:, 0:H, q], yf[:, :, :], xh32[:, 0:H, q], ALU.subtract).then_inc(yl_done, 1)
                    dve.wait_ge(yl_done, Y0[l] + 4 + t + 1)

                for k in range(len(us) + 7):
                    if k < len(us):
                        unit_max(k)
                    if 1 <= k <= len(us):
                        unit_dif(k - 1)
                    if k < 4:
                        dve.wait_ge(yh_done, Y0[l] + k + 1)
                        dve.tensor_tensor(xl[:, 4 + k, 0:w], cx[:, ysrc[k], 0:w], xh32[:, 4 + k, 0:w], ALU.subtract)\
                            .then_inc(yl_done, 1)
                    if k >= 7 and (k - 7) % H == 0 and (k - 7) // H < NT[l]:
                        tile_out((k - 7) // H)
                    if k >= 9 and (k - 9) % H == 0 and (k - 9) // H < NT[l]:
                        tile_scale((k - 9) // H)
                    if k >= 10 and (k - 10) % H == 0 and (k - 10) // H < NT[l]:
                        tile_low((k - 10) // H)
                m = 3 * l + 1
                gate_columns(m)
                for d in range(OB):
                    n = n0 + CV + VB + d
                    if d < OB - 1:
                        split_next(n)
                    dve.wait_ge(block_done, n + 1)
                    update(m, d, d % 4)
                    if d >= 1:
                        add_square(m + 1, d - 1)
                split_next(n0 + CV + VB + OB - 1)
                norm(m + 1)

            dve.wait_ge(cols_in, 16)
            dve.memset(ps[:, 5, :], 0.0).then_inc(rows_zero, 1)
            for d in range(DC - 1):
                add_square(0, d)
            dve.wait_ge(rows_done, 1)
            dve.tensor_copy(wm0_rows[:, :], ps[:, 5, :]).then_inc(rows_out, 1)
            dve.wait_ge(mod_sum, START_UNITS)
            turned = ps[:, 6, 0:START_UNITS * UC].rearrange("p (j u v) -> p u j v", u=START_UNITS, v=2)
            bias = col("b_mod", 0, START_UNITS * UC).rearrange("p (u j v) -> p u j v", u=START_UNITS, v=2)
            flat = modc[:, :, :, :].rearrange("p a b c -> p (a b c)")[:, 0:START_UNITS * UC]
            dve.tensor_tensor(flat.rearrange("p (u j v) -> p u j v", u=START_UNITS, v=2), turned, bias, ALU.add)\
                .then_inc(mod_col, START_UNITS)
            dve.wait_ge(mod_col, START_UNITS)
            split(0)
            split(1)
            norm(0)
            dve.wait_ge(cols2_in, 16)
            for l in range(DEPTH):
                for b in range(2):
                    a = l * 4 * DH + 2 * b * DH
                    own(dve.tensor_tensor(lamt[:, b, :], col("lam", a, DH), col("lam", a + DH, DH), ALU.mult))
                    own(dve.tensor_reduce(lamc[:, l, b:b + 1], lamt[:, b, :], AX.X, ALU.add))
            dve.sem_inc(lam_red, 1)
            dve.wait_ge(lam_exp, 1)
            for l in range(DEPTH):
                own(dve.tensor_tensor(lamc[:, l, 4:5], lamc[:, l, 3:4], lamc[:, l, 2:3], ALU.subtract))
                own(dve.tensor_scalar(lamc[:, l, 5:6], lamc[:, l, 4:5], lam_init[l], None, ALU.subtract))
                own(dve.tensor_scalar(lamc[:, l, 6:7], col("subln", l), 1.0 - lam_init[l], None, ALU.mult))
            for l in range(DEPTH):
                ffn(l, 0)
                mixer(l)
                ffn(l, 2)

        @block.tensor
        def _(pe):
            def three(out_ap, hi_w, lo_w, hi_x, lo_x, start, stop):
                pe.matmul(out_ap, hi_w, hi_x, start=start, stop=False)
                pe.matmul(out_ap, hi_w, lo_x, start=False, stop=False)
                return pe.matmul(out_ap, lo_w, hi_x, start=False, stop=stop)

            def column_block(n, bank, w, i=0, k=0, order=range(DC), ready=None, a=0, last=True):
                pe.wait_ge(lo_done, i * (4 * k) + (n + 1))
                for q, c in enumerate(order):
                    if ready and c in ready:
                        pe.wait_ge(*ready[c])
                    ins = three(ps[:, bank, a:w], whi[:, n % SPL, c, :], wlo[:, n % SPL, c, :],
                                xh[:, c, a:w], xl[:, c, a:w], q == 0, q == DC - 1)
                if last:
                    ins.then_inc(block_done, 1)

            def first_blocks(m, n):
                for s in range(streams(m)):
                    for q in range(2):
                        ready = {c: (xl_done, xstep(m, c, s)) for c in range(DC)} if q == 0 else None
                        column_block(n + q, q, (s + 1) * S, ready=ready, a=s * S, last=s == streams(m) - 1)

            def mod_start():
                pe.wait_ge(cs_done, 1)
                pe.wait_ge(rows_zero, 1)
                for c in range(DC):
                    if c % 2 == 0:
                        pe.wait_ge(wm0_in[c // 2], 16)
                    for u in range(START_UNITS):
                        ins = pe.matmul(ps[32 * u:32 * u + 2, 5, :], cs[:, 2 * c:2 * c + 2],
                                        wm0[:, c // 2, u, c % 2, :], start=c == 0, stop=c == DC - 1)
                ins.then_inc(rows_done, 1)
                pe.wait_ge(rows_out, 1)
                for j in range(HN // P):
                    ins = pe.matmul(ps[:, 6, 8 * j:8 * j + 8], wm0_rows[:, j * P:(j + 1) * P], col("sel", 0, 8),
                                    start=True, stop=True)
                ins.then_inc(mod_sum, START_UNITS)

            def mod_sums(u, i=0):
                pe.wait_ge(mod_acc, i * (2 * DC) + unit_steps(u + 1))
                pe.wait_ge(mod_col, i + u)
                for c in range(HN // P):
                    for v in range(2):
                        ins = pe.matmul(ps[:, 5, 2 * c + v:2 * c + v + 1], macc[:, v, c * P:(c + 1) * P],
                                        col("one", 0, 1), start=True, stop=True)
                ins.then_inc(mod_sum, 1)

            def norm_stat(m):
                w = width(m)
                pe.wait_ge(ssq_done, (DC - 1) * (m + 1))
                pe.matmul(ps[:, 4, 0:w], col("ones", 0, P), ssq[:, 0:w], start=True, stop=False)
                pe.wait_ge(sq_done, DC * (m + 1))
                pe.matmul(ps[:, 4, 0:w], col("ones", 0, P), sq[:, (DC - 1) % 2, 0:w], start=False, stop=True)\
                    .then_inc(stat_done, 1)

            def ffn(l, st):
                f = 2 * l + (st == 2)
                m = 3 * l + st
                n0 = PER_LAYER * l + (0 if st == 0 else FFN + MIX)
                w = width(m)
                u0, nu = UNIT_AT.get(f, (0, 0))
                F0 = FC * f

                def body(i, sums, first=False):
                    if first:
                        first_blocks(m, n0)
                    for e in range(2 if first else 0, 4):
                        if e % 2 == 0 and not first:
                            pe.wait_ge(mul_done, i * 2 + (F0 + e // 2 - 1))
                        column_block(n0 + e, e, w, i, 1)
                        if e == 0 and sums:
                            mod_sums(u0 - 1, i)

                body(0, False, True)
                if nu:
                    with pe.Fori(1, min(nu + 1, GU // 4)) as i:
                        body(i, True)
                if nu + 1 < GU // 4:
                    with pe.Fori(nu + 1, GU // 4) as i:
                        body(i, False)
                if nu == GU // 4:
                    mod_sums(u0 + nu - 1)
                for hf in range(2):
                    nd = n0 + GU + HALF * hf
                    b0 = 4 if hf == 0 else 0

                    def down(b, i=0, k=0):
                        n = nd + b
                        pe.wait_ge(lo_done, i * (4 * k) + (n + 1))
                        if hf == 0:
                            pe.wait_ge(al_done, i * (8 * k) + (F0 + 2 * b + 2))
                        last = b == HALF - 1 and hf == 1
                        for r, d in [(r, d) for d in range(4) for r in range(2)] if last else \
                                [(r, d) for r in range(2) for d in range(4)]:
                            src = bass.ds(i * (8 * T * k) + (2 * b + r) * T, w)
                            ins = three(ps[:, b0 + d, 0:w], whi[:, n % SPL, 4 * r + d, :],
                                        wlo[:, n % SPL, 4 * r + d, :], ah[:, src], al[:, src],
                                        b == 0 and r == 0, b == HALF - 1 and r == 1)
                            if last and r == 1 and d < 3:
                                ins.then_inc(dn_done, 1)
                        ins.then_inc(block_done, 1)

                    if hf == 0 and nu:
                        pe.wait_ge(mod_col, u0 + nu)
                    down(0)
                    with pe.Fori(0, (HALF - 3) // 4) as i:
                        for e in range(4):
                            down(1 + e, i, 1)
                    down(HALF - 2)
                    down(HALF - 1)
                if m + 1 < 6:
                    norm_stat(m + 1)

            def mixer(l):
                n0, w = B_win[l], ntile(l)
                m = 3 * l + 1

                def stat(b):
                    qk, wb = 8 * l + b, T if b < 4 else w
                    pe.wait_ge(sqk_done, qk + 1)
                    if b >= 2:
                        pe.wait_ge(rq_done, qk - 1)
                    pe.matmul(ps[:, 6 + b % 2, 0:wb], col("halves", 0, P), sqk[:, b % 2, 0:wb], start=True, stop=True)\
                        .then_inc(qk_stat, 1)

                first_blocks(m, n0)
                for b in range(1, QKB + CB):
                    if b >= 4:
                        pe.wait_ge(evac, EV[l] + b - 3)
                        if b - 4 < QKB:
                            pe.wait_ge(sqk_done, 8 * l + b - 3)
                    if b >= 2:
                        column_block(n0 + b, b % 4, T if b < 4 else w)
                    if 1 <= b <= QKB:
                        stat(b - 1)
                    if l == 0 and b == QKB + PAIRS + 1:
                        mod_sums(MIX_UNIT)
                pe.wait_ge(rq_done, 8 * (l + 1))
                if l == 0:
                    pe.wait_ge(mod_col, MIX_UNIT + 1)
                for b in range(VB):
                    n = n0 + CV + b
                    pe.wait_ge(lo_done, n + 1)
                    for r in range(2):
                        c = 2 * b + r
                        wh = whi[:, n % SPL, 4 * r:4 * r + 4, :].rearrange("p a b -> p (a b)")
                        wl = wlo[:, n % SPL, 4 * r:4 * r + 4, :].rearrange("p a b -> p (a b)")
                        for t in range(4):
                            ins = three(ps[:, 4 + t, :], xh[:, c, t * P:(t + 1) * P], xl[:, c, t * P:(t + 1) * P],
                                        wh, wl, c == 0, c == DC - 1)
                    ins.then_inc(block_done, 1)
                    if b >= 2:
                        c = b - 2
                        pe.wait_ge(pooled_done, 2 * l + c + 1)
                        pe.wait_ge(evac, EV[l] + 16)
                        pe.matmul(ps[:, c, 0:w], col("poolw", (2 * l + c) * P, P), pooled[:, c, 0:w],
                                  start=True, stop=True).then_inc(pool_mm, 1)
                us = units(l)
                pe.wait_ge(qk_ready, 8 * (l + 1))
                pe.wait_ge(y_done, Y0[l] + 4)

                def scores(k):
                    t, hd = us[k]
                    u = U0[l] + k
                    a, wk = (0, T) if t < 2 else (S, S)
                    if k >= 2:
                        pe.wait_ge(exp_done, 2 * (u - 1))
                    for b in range(2):
                        pr = slice(64 * b, 64 * b + 64)
                        ins = pe.matmul(ps[:, 2 * (u % 2) + b, 0:wk], kq[pr, 4 + hd, t * P:(t + 1) * P],
                                        kq[pr, hd, a:a + wk], start=True, stop=True)
                    ins.then_inc(score_done, 1)

                def turn(k):
                    u = U0[l] + k
                    nk = 4 if us[k][0] < 2 else 2
                    pe.wait_ge(dif_done, u + 1)
                    if k == 0:
                        pe.wait_ge(evac, EV[l] + 20)
                    if k >= 2:
                        pe.wait_ge(difT_done, u - 1)
                    for j in range(nk):
                        ins = pe.transpose(ps[:, 4 + u % 2, j * P:(j + 1) * P], att[:, u % 2, j * P:(j + 1) * P],
                                           col("ident", 0, P))
                    ins.then_inc(tr_done, 1)

                def values(k):
                    t, hd = us[k]
                    u = U0[l] + k
                    k0, nk = (0, 4) if t < 2 else (2, 2)
                    pe.wait_ge(difT_done, u + 1)
                    if hd == 0 and t >= 2:
                        pe.wait_ge(orstd, TB[l] + t - 1)
                    for j in range(nk):
                        ins = pe.matmul(ps[:, 6 + t % 2, hd * P:(hd + 1) * P], vt[:, k0 + j, hd * P:(hd + 1) * P],
                                        difT[:, u % 2, j, :], start=(j == 0), stop=(j == nk - 1))
                    ins.then_inc(pv_done, 1)

                def tile_stat(t):
                    g = TB[l] + t
                    pe.wait_ge(osq_done, g + 1)
                    pe.matmul(ps[:, 6 + t % 2, :], col("ones", 0, P), sqk[:, g % 2, :], start=True, stop=True)\
                        .then_inc(ostat, 1)

                for k in range(len(us) + 6):
                    if k < len(us):
                        scores(k)
                    if k >= 8 and (k - 8) % H == 0 and (k - 8) // H < NT[l]:
                        tile_stat((k - 8) // H)
                    if 2 <= k <= len(us) + 1:
                        turn(k - 2)
                    if 3 <= k <= len(us) + 2:
                        values(k - 3)
                order = (4, 5, 6, 7, 0, 1, 2, 3)
                ready = {4: (yl_done, Y0[l] + 4), 0: (yl_done, Y0[l] + 4 + NT[l])}
                for d in range(OB):
                    n = n0 + CV + VB + d
                    if d >= 4:
                        pe.wait_ge(h_done, DC * (3 * l + 1) + d - 3)
                    column_block(n, d % 4, w, order=order, ready=ready if d == 0 else None)
                norm_stat(3 * l + 2)

            pe.wait_ge(cols_in, 16)
            norm_stat(0)
            mod_start()
            for l in range(DEPTH):
                ffn(l, 0)
                mixer(l)
                ffn(l, 2)


def blocks_of(w, rows_per_block, col_chunks):
    k, n = w.shape
    a = w.reshape(k // (rows_per_block * P), rows_per_block, P, n // (col_chunks * P), col_chunks * P)
    a = a.transpose(3, 0, 2, 1, 4)
    return a.reshape(-1, P, BLK)


def kernel(x, c, ctx, c_ctx, norm_w, w_mod, b_mod, ffn1_w_gu, ffn1_w_down, ffn2_w_gu, ffn2_w_down,
           w_in, w_out, q_norm_w, k_norm_w, lambda_qk, subln_w, conv_w, pool_w, pool_scale):
    import concourse.bacc as bacc
    from concourse.bass_utils import run_bass_kernel_spmd

    f = lambda a: np.asarray(a)
    stream = []
    for l in range(DEPTH):
        def ffn_blocks(gu, dn):
            g = blocks_of(f(gu)[l], DC, 1)
            return [np.stack([g[:FC], g[FC:]], 1).reshape(-1, P, BLK), blocks_of(f(dn)[l], 2, 4)]
        stream += ffn_blocks(ffn1_w_gu, ffn1_w_down)
        wi = f(w_in)[l]
        W, C = 4 * P, 2 * P
        q, k, v, cb, cc, cxx, pu = (wi[:, a:b] for a, b in
                                    ((0, W), (W, 2 * W), (2 * W, 3 * W), (3 * W, 3 * W + C),
                                     (3 * W + C, 3 * W + 2 * C), (3 * W + 2 * C, 3 * W + 3 * C),
                                     (3 * W + 3 * C, 3 * W + 4 * C)))
        stream += [blocks_of(a, DC, 1) for a in (k, q, cc, cxx, cb, pu)] + [blocks_of(v, 2, 4)]
        stream += [blocks_of(f(w_out)[l], DC, 1)]
        stream += ffn_blocks(ffn2_w_gu, ffn2_w_down)
    wstream = np.concatenate(stream)
    assert wstream.shape[0] == NB
    wmod = np.ascontiguousarray(f(w_mod).reshape(DEPTH, PAIRS, 2, P, 2 * N_MOD, HN).transpose(0, 4, 1, 3, 2, 5)
                                .reshape(UNITS * PAIRS, P, 2 * HN))

    def two(a):
        a = a.reshape(-1, DC, P).transpose(2, 0, 1)
        return np.repeat(a[..., None], 2, -1).reshape(P, -1)

    nf = DH // 4
    inv = 10000.0 ** (-np.arange(nf, dtype=np.float32) / nf)
    t = np.arange(S)
    ang = np.stack([(t // GRID_W)[:, None] * inv, (t % GRID_W)[:, None] * inv], 1).astype(np.float32)
    cos = np.repeat(np.cos(ang)[:, :, None], 2, 2).reshape(S, DH).T
    sin = np.stack([-np.sin(ang), np.sin(ang)], 2).reshape(S, DH).T
    win = np.repeat(np.array(WINDOWS), DH)[:, None]
    cnt = np.minimum(t + win // 2, S) - np.maximum(t - win // 2, 0)
    pw = np.zeros((DEPTH, 2, P, P), np.float32)
    for g in range(4):
        a = slice(64 * (g % 2), 64 * (g % 2) + 64)
        pw[:, g // 2, a, a] = f(pool_w)[:, g]
    pieces = {
        "c": np.stack([f(c)[0], f(c_ctx)], -1).reshape(DC, P, 2).transpose(1, 0, 2).reshape(P, -1),
        "norm_w": two(f(norm_w)),
        "b_mod": two(f(b_mod)),
        "qw": np.tile(f(q_norm_w).T, (2, 1)),
        "kw": np.tile(f(k_norm_w).T, (2, 1)),
        "subln": f(subln_w).T,
        "conv": f(conv_w).reshape(DEPTH, 3, 2, P).transpose(3, 0, 2, 1).reshape(P, -1),
        "pscale": f(pool_scale).reshape(DEPTH * 2, P).T,
        "lam": np.broadcast_to(f(lambda_qk).reshape(1, -1), (P, DEPTH * 4 * DH)),
        "eps": np.full((P, 1), EPS),
        "one": np.ones((P, 1)),
        "sel": np.stack([np.arange(P) == 32 * u + v for u in range(4) for v in range(2)], 1),
        "cos": np.tile(cos, (2, 1)),
        "sin": np.tile(sin, (2, 1)),
        "rcnt": (1.0 / cnt).reshape(2, P, S).transpose(1, 0, 2).reshape(P, -1),
        "ones": np.ones((P, P)),
        "halves": np.kron(np.eye(2), np.ones((DH, DH))),
        "ident": np.eye(P),
        "poolw": pw.transpose(2, 0, 1, 3).reshape(P, -1),
    }
    cols = np.zeros((P, NCOL), np.float32)
    for name, (a, n) in COLS.items():
        cols[:, a:a + n] = pieces[name]
    x_t = np.ascontiguousarray(np.concatenate([f(x)[0], f(ctx)[0]]).T)

    nc = bacc.Bacc("TRN2", target_bir_lowering=False, num_devices=1)
    arrays = {"wstream": wstream, "wmod": wmod, "cols": cols, "x_t": x_t}
    aps = {n: nc.dram_tensor(n, a.shape, F32, kind="ExternalInput").ap() for n, a in arrays.items()}
    out = nc.dram_tensor("out_t", (D, S), F32, kind="ExternalOutput").ap()
    program(nc, aps["wstream"], aps["wmod"], aps["cols"], aps["x_t"], out)
    r = run_bass_kernel_spmd(nc, [arrays], core_ids=[0])
    return np.ascontiguousarray(r.results[0]["out_t"].T)[None]
```

```python
import math
from contextlib import ExitStack

import numpy as np
import concourse.bass as bass
from concourse import mybir
from concourse.alu_op_type import AluOpType as ALU

F32, F32R = mybir.dt.float32, mybir.dt.float32r
ACT = mybir.ActivationFunctionType
AX = mybir.AxisListType

P = 128
D = 1024
DC = D // P
S = 256
T = 2 * S
DEPTH = 2
F_FF = 2816
FC = F_FF // P
H = 4
DH = 64
N_MOD = 9
EPS = 1e-6
WINDOWS = (2, 4, 8, 16)
GRID_W = 64
PADW = 8
PW = S + 2 * PADW

TILES = 8
BLK = TILES * P
RAW = 4
SPL = 2
GU = 2 * FC
DN = FC
HALF = DN // 2
QKB, CB, VB, OB = 8, 8, 4, 8
CV = QKB + CB
FFN = GU + DN
MIX = VB + QKB + CB + OB
PER_LAYER = 2 * FFN + MIX
NB = DEPTH * PER_LAYER

HN = D // 2
PAIRS = DC // 2
UNITS = DEPTH * N_MOD * 2
UC = HN // P * 2
START_UNITS = 4
UNIT_AT = {0: (4, GU // 4), 1: (16, GU // 4), 2: (27, 9)}
MIX_UNIT = 15

COLS = {}
_at = 0
for _name, _n in (("c", DC * 2), ("norm_w", DEPTH * 3 * DC * 2), ("b_mod", DEPTH * N_MOD * DC * 2),
                  ("eps", 1), ("one", 1), ("sel", 8), ("ones", P),
                  ("qw", DEPTH), ("kw", DEPTH), ("subln", DEPTH), ("conv", DEPTH * 2 * 3),
                  ("pscale", DEPTH * 2), ("lam", DEPTH * 4 * DH),
                  ("cos", S), ("sin", S), ("rcnt", 2 * S), ("halves", P),
                  ("ident", P), ("poolw", DEPTH * 2 * P)):
    COLS[_name] = (_at, _n)
    _at += _n
NCOL = _at
EARLY = COLS["qw"][0]


def program(nc, wstream, wmod, cols, x_t, out):
    with ExitStack() as ctx:
        def sb(name, shape, dt=F32):
            return ctx.enter_context(nc.sbuf_tensor(name, shape, dt))

        def sem(name):
            return ctx.enter_context(nc.semaphore(name))

        raw = sb("raw", [P, RAW, BLK])
        whi = sb("whi", [P, SPL, TILES, P], F32R)
        wlo = sb("wlo", [P, SPL, TILES, P], F32R)
        h = sb("h", [P, DC, T])
        xh = sb("xh", [P, DC, T], F32R)
        xl = sb("xl", [P, DC, T], F32R)
        xh32 = xh[:, :, :].bitcast(F32)
        wm = sb("wm", [P, 2, 2, HN])
        K = sb("K", [P, NCOL])
        cs = sb("cs", [P, DC * 2])
        modc = sb("modc", [P, DEPTH * N_MOD, DC, 2])
        acol = sb("acol", [P, DEPTH * 3, DC, 2])
        gcol = sb("gcol", [P, DEPTH * 3, DC, 2])
        lamc = sb("lamc", [P, DEPTH, 8])
        qws = sb("qws", [P, DEPTH])
        lamt = sb("lamt", [P, 2, DH])
        shared_a = sb("shared_a", [P, 3 * T])
        macc = shared_a[:, 0:2 * HN].rearrange("p (v n) -> p v n", v=2)
        sq = shared_a[:, 0:2 * T].rearrange("p (a t) -> p a t", a=2)
        ssq = shared_a[:, 2 * T:3 * T]
        shared_b = sb("shared_b", [P, 4 * T])
        sil = shared_b[:, 0:2 * T].rearrange("p (a t) -> p a t", a=2)
        af = shared_b[:, 2 * T:4 * T].rearrange("p (a t) -> p a t", a=2)
        lnv = shared_b[:, 0:T]
        rstd = shared_b[:, T:2 * T]
        xt = shared_b[:, 2 * T:4 * T].rearrange("p (a t) -> p a t", a=4)
        hidden = ExitStack()
        ah = hidden.enter_context(nc.sbuf_tensor("ah", [P, FC * T], F32R))
        al = hidden.enter_context(nc.sbuf_tensor("al", [P, FC * T], F32R))
        hidden.close()
        wm0_place = ExitStack()
        wm0 = wm0_place.enter_context(nc.sbuf_tensor("wm0", [P, PAIRS, START_UNITS, 2, HN], F32))
        wm0_rows = wm0_place.enter_context(nc.sbuf_tensor("wm0_rows", [P, HN], F32))
        wm0_place.close()
        kq = sb("kq", [P, 8, T])
        vt = sb("vt", [P, 4, T])
        cx = sb("cx", [P, 8, T])
        sqk = sb("sqk", [P, 2, T])
        lnk = sb("lnk", [P, T])
        rq = sb("rq", [P, 2, T])
        shf = sb("shf", [P, S])
        rot = sb("rot", [P, S])
        prob = sb("prob", [P, 2, 2, T])
        att = sb("att", [P, 3, T])
        difT = sb("difT", [P, 2, 4, P])
        nmax = sb("nmax", [P, 2, 2])
        lsum = sb("lsum", [P, 2, 2])
        linv = sb("linv", [P, 2, 2])
        nlin = sb("nlin", [P, 2, 1])
        of = sb("of", [P, 2, H, P])
        pad0 = sb("pad0", [P, 2, PW])
        pad1 = sb("pad1", [P, 2, PW])
        pooled = cx[:, 0:2, :]
        ysrc = (4, 5, 0, 1)
        Z = (2, 3, 6, 7)
        box = cx[:, 2:4, :].rearrange("p c (s t) -> p c s t", t=S)
        cu = sb("cu", [P, 2, 2, S + 2])
        cy = sb("cy", [P, 2, S])
        ps = ctx.enter_context(nc.psum_tensor("ps", [P, 8, T], F32))

        def col(name, i=0, n=1):
            a = COLS[name][0] + i
            assert i + n <= COLS[name][1]
            return K[:, a:a + n]

        cols_in = sem("cols_in")
        x_in = sem("x_in")
        raw_in = [sem(f"raw_in{i}") for i in range(RAW)]
        hi_done = sem("hi_done")
        lo_done = sem("lo_done")
        block_done = sem("block_done")
        wm_in = [sem(f"wm_in{i}") for i in range(2)]
        cs_done = sem("cs_done")
        cols2_in = sem("cols2_in")
        wm0_in = [sem(f"wm0_in{p}") for p in range(PAIRS + 1)]
        rows_zero = sem("rows_zero")
        rows_done = sem("rows_done")
        rows_out = sem("rows_out")
        wm_used = sem("wm_used")
        mod_acc = sem("mod_acc")
        mod_sum = sem("mod_sum")
        mod_col = sem("mod_col")
        dn_done = sem("dn_done")
        h_done = sem("h_done")
        sq_done = sem("sq_done")
        ssq_done = sem("ssq_done")
        stat_done = sem("stat_done")
        ln_done = sem("ln_done")
        rstd_done = sem("rstd_done")
        xt_done = sem("xt_done")
        xh_done = sem("xh_done")
        xl_done = sem("xl_done")
        silu_done = sem("silu_done")
        mul_done = sem("mul_done")
        ah_done = sem("ah_done")
        al_done = sem("al_done")
        evac = sem("evac")
        sqk_done = sem("sqk_done")
        qk_stat = sem("qk_stat")
        lnk_done = sem("lnk_done")
        rq_done = sem("rq_done")
        qk_used = sem("qk_used")
        qk_ready = sem("qk_ready")
        q_copied = sem("q_copied")
        q_zero = sem("q_zero")
        q_ready = sem("q_ready")
        score_done = sem("score_done")
        max_done = sem("max_done")
        exp_done = sem("exp_done")
        dif_done = sem("dif_done")
        tr_done = sem("tr_done")
        difT_done = sem("difT_done")
        pv_done = sem("pv_done")
        of_done = sem("of_done")
        osq_done = sem("osq_done")
        ostat = sem("ostat")
        orstd = sem("orstd")
        oln = sem("oln")
        y_done = sem("y_done")
        yh_done = sem("yh_done")
        yl_done = sem("yl_done")
        pooled_done = sem("pooled_done")
        pool_mm = sem("pool_mm")
        dve_step = sem("dve_step")
        lam_red = sem("lam_red")
        lam_exp = sem("lam_exp")
        out_sem = sem("out_sem")

        def width(m):
            return T if m < 5 else S

        def streams(m):
            return width(m) // S

        ADDED = DC - 2

        XT = [2 * DC * m for m in range(7)]

        def xstep(m, d, s):
            return XT[m] + DC * s + d + 1

        def units(l):
            return [(t, hd) for t in range(4 if l == 0 else 2) for hd in range(H)]

        U0 = [0, 4 * H]
        EV = [0, 20]

        def ntile(l):
            return T if l == 0 else S

        NT = [4, 2]
        TB = [0, 4]
        Y0 = [0, 8]

        def tile_at(l, k, after):
            return k >= after and (k - after) % H == 0 and (k - after) // H < NT[l] - (2 if after > 8 else 1)

        def unit_steps(u):
            return 2 * DC * (u - START_UNITS)
        B_win = [PER_LAYER * l + FFN for l in range(DEPTH)]
        lam_init = [0.8 - 0.6 * math.exp(-0.3 * l) for l in range(DEPTH)]

        block = ctx.enter_context(nc.Block())

        @block.sync
        def _(sp):
            sp.dma_start(K[:, 0:EARLY], cols[:, 0:EARLY]).then_inc(cols_in, 16)
            sp.dma_start(h[:, :, :], x_t.rearrange("(c p) t -> p c t", p=P)).then_inc(x_in, 16)
            start_pairs = wmod[0:START_UNITS * PAIRS].rearrange("(u q) p n -> q p u n", q=PAIRS)
            for p in range(PAIRS - 1):
                sp.dma_start(wm0[:, p, :, :, :].rearrange("p u a n -> p u (a n)"), start_pairs[p])\
                    .then_inc(wm0_in[p], 16)
            for r in range(2):
                sp.dma_start(wm0[:, PAIRS - 1, :, r, :], start_pairs[PAIRS - 1][:, :, r * HN:(r + 1) * HN])\
                    .then_inc(wm0_in[PAIRS - 1 + r], 16)
            for n in range(RAW):
                sp.dma_start(raw[:, n, :], wstream[n]).then_inc(raw_in[n], 16)
                if n == 1:
                    sp.dma_start(K[:, EARLY:NCOL], cols[:, EARLY:NCOL]).then_inc(cols2_in, 16)
            with sp.Fori(1, NB // RAW) as i:
                for s in range(RAW):
                    sp.wait_ge(lo_done, i * RAW + (s + 1 - RAW))
                    sp.dma_start(raw[:, s, :], wstream[bass.ds(i * RAW + s, 1)].rearrange("a p n -> p (a n)"))\
                        .then_inc(raw_in[s], 16)
            for d in range(DC):
                sp.wait_ge(h_done, 5 * DC + d + 1)
                sp.dma_start(out[d * P:(d + 1) * P, :], h[:, d, 0:S]).then_inc(out_sem, 16)
            sp.wait_ge(out_sem, 16 * DC)

        @block.gpsimd
        def _(pool):
            u0 = START_UNITS * PAIRS
            for c in range(2):
                pool.dma_start(wm[:, c, :, :].rearrange("p a n -> p (a n)"), wmod[u0 + c]).then_inc(wm_in[c], 16)

            def loads(a, b):
                with pool.Fori(a, b) as i:
                    for c in range(2):
                        pool.wait_ge(wm_used, i * 2 + (c - 1 - u0))
                        pool.dma_start(wm[:, c, :, :].rearrange("p a n -> p (a n)"),
                                       wmod[bass.ds(i * 2 + c, 1)].rearrange("a p n -> p (a n)"))\
                            .then_inc(wm_in[c], 16)

            def query_zeros(l):
                pool.wait_ge(pooled_done, 2 * (l + 1))
                for a in range(2):
                    ins = pool.memset(cx[0:DH, Z[2 * a]:Z[2 * a] + 2, 0:ntile(l)], 0.0)
                ins.then_inc(q_zero, 1)

            def conv_pool_low(l):
                w = ntile(l)
                for k in range(4):
                    pool.wait_ge(yh_done, Y0[l] + k + 1)
                    pool.tensor_tensor(xl[:, 4 + k, 0:w], cx[:, ysrc[k], 0:w], xh32[:, 4 + k, 0:w],
                                       ALU.subtract).then_inc(yl_done, 1)

            after_mix = (MIX_UNIT + 1) * PAIRS // 2 + 1
            loads(u0 // 2 + 1, after_mix)
            query_zeros(0)
            conv_pool_low(0)
            loads(after_mix, UNITS * PAIRS // 2)
            query_zeros(1)
            conv_pool_low(1)

        @block.scalar
        def _(act):
            def split(n, i=0, k=0):
                s = n % RAW
                act.wait_ge(raw_in[s], i * (16 * k) + 16 * (n // RAW + 1))
                if n >= SPL:
                    act.wait_ge(block_done, i * (4 * k) + (n - SPL + 1))
                act.activation(whi[:, n % SPL, :, :].rearrange("p a b -> p (a b)"), raw[:, s, :], ACT.Copy)\
                    .then_inc(hi_done, 1)

            def split_next(n, i=0, k=0):
                if n + SPL < NB:
                    split(n + SPL, i, k)

            def silu(f, j, j0, i, n, w):
                F0 = FC * f
                act.wait_ge(block_done, i * 4 + (n + 1))
                if F0 + j0 >= 2:
                    act.wait_ge(mul_done, i * 2 + (F0 + j - 1))
                act.activation(sil[:, j % 2, 0:w], ps[:, 2 * (j % 2), 0:w], ACT.Silu).then_inc(silu_done, 1)

            def hidden_high(f, j, i, w):
                act.wait_ge(mul_done, i * 2 + (FC * f + j + 1))
                act.activation(ah[:, bass.ds(i * (2 * T) + j * T, w)], af[:, j % 2, 0:w], ACT.Copy)\
                    .then_inc(ah_done, 1)

            def ffn(l, st):
                f = 2 * l + (st == 2)
                n0 = PER_LAYER * l + (0 if st == 0 else FFN + MIX)
                w = width(3 * l + st)

                def body(i, j0):
                    for e in range(4):
                        split_next(n0 + e, i, 1)
                        if e % 2:
                            silu(f, e // 2, j0 + e // 2, i, n0 + e, w)
                        elif e or j0:
                            hidden_high(f, e // 2 - 1, i, w)

                body(0, 0)
                with act.Fori(1, GU // 4) as i:
                    body(i, 2)
                hidden_high(f, -1, GU // 4, w)
                m = 3 * l + st + 1
                for hf in range(2):
                    nd = n0 + GU + HALF * hf
                    split_next(nd)
                    with act.Fori(0, (HALF - 3) // 4) as i:
                        for e in range(4):
                            split_next(nd + 1 + e, i, 1)
                    split_next(nd + HALF - 2)
                    if hf == 0:
                        split_next(nd + HALF - 1)
                    if m < 6:
                        if hf == 1:
                            ln_exp_tables()
                        for d in range(4 * hf, 4 * hf + 4):
                            square(m, d)
                    if hf == 1:
                        split_next(nd + HALF - 1)
                if m < 6:
                    norm(m)

            def ln_exp_tables():
                act.preload_act_table_set("natural_log_exp_and_others")

            def square(m, d):
                w = width(m)
                g = DC * m + d
                if m == 0:
                    if d == 0:
                        act.wait_ge(x_in, 16)
                else:
                    act.wait_ge(h_done, DC * (m - 1) + d + 1)
                if d >= 2:
                    act.wait_ge(ssq_done, ADDED * m + d - 1)
                elif m > 0:
                    act.wait_ge(stat_done, m)
                act.activation(sq[:, g % 2, 0:w], h[:, d, 0:w], ACT.Square).then_inc(sq_done, 1)

            def norm(m):
                w = width(m)
                act.wait_ge(stat_done, m + 1)
                for s in range(streams(m)):
                    a, g = slice(s * S, (s + 1) * S), 2 * m + s + 1
                    act.activation(lnv[:, a], ps[:, 4, a], ACT.Ln, bias=col("eps"), scale=1.0 / D)\
                        .then_inc(ln_done, 1)
                    act.wait_ge(ln_done, g)
                    act.activation(rstd[:, a], lnv[:, a], ACT.Exp, scale=-0.5).then_inc(rstd_done, 1)
                l, st = divmod(m, 3)
                for s in range(streams(m)):
                    for d in range(DC):
                        g = xstep(m, d, s)
                        act.wait_ge(xt_done, g)
                        act.activation(xh[:, d, s * S:(s + 1) * S], xt[:, (g - 1) % 4, :], ACT.Identity,
                                       bias=modc[:, N_MOD * l + 3 * st, d, s:s + 1]).then_inc(xh_done, 1)

            def mixer(l):
                n0, w = B_win[l], ntile(l)

                def wid(b):
                    return T if b < 4 else w

                for b in range(QKB + CB):
                    split_next(n0 + b)
                    if l == 0 and b == 1:
                        act.wait_ge(lam_red, 1)
                        act.activation(lamc[:, :, 2:4], lamc[:, :, 0:2], ACT.Exp).then_inc(lam_exp, 1)
                    act.wait_ge(block_done, n0 + b + 1)
                    dst = kq[:, b, 0:wid(b)] if b < QKB else cx[:, b - QKB, 0:w]
                    act.activation(dst, ps[:, b % 4, 0:wid(b)], ACT.Copy).then_inc(evac, 1)
                    if b < QKB:
                        if b >= 2:
                            act.wait_ge(qk_stat, 8 * l + b - 1)
                        act.activation(sqk[:, b % 2, 0:wid(b)], ps[:, b % 4, 0:wid(b)], ACT.Square)\
                            .then_inc(sqk_done, 1)
                    if 1 <= b <= QKB:
                        qk, c = 8 * l + b - 1, b - 1
                        act.wait_ge(qk_stat, qk + 1)
                        if qk >= 1:
                            act.wait_ge(rq_done, qk)
                        act.activation(lnk[:, 0:wid(c)], ps[:, 6 + c % 2, 0:wid(c)], ACT.Ln, bias=col("eps"),
                                       scale=1.0 / DH).then_inc(lnk_done, 1)
                        act.wait_ge(lnk_done, qk + 1)
                        if c >= 2:
                            act.wait_ge(qk_used, qk - 1)
                        act.activation(rq[:, c % 2, 0:wid(c)], lnk[:, 0:wid(c)], ACT.Exp, scale=-0.5)\
                            .then_inc(rq_done, 1)
                for b in range(VB - 1):
                    split_next(n0 + CV + b)
                    if b == 1:
                        act.wait_ge(pooled_done, 2 * (l + 1))
                        act.wait_ge(qk_ready, 8 * (l + 1))
                        for a in range(2):
                            ins = act.activation(cx[DH:P, Z[2 * a]:Z[2 * a] + 2, 0:w],
                                                 kq[DH:P, H + 2 * a:H + 2 * a + 2, 0:w], ACT.Copy)
                        ins.then_inc(q_copied, 1)
                act.wait_ge(block_done, n0 + CV + VB)

                def copy_v(cs):
                    for c in cs:
                        act.activation(vt[:, c, :], ps[:, 4 + c, :], ACT.Copy).then_inc(evac, 1)

                copy_v((0, 1))
                us = units(l)

                def unit_exp(k):
                    t, _ = us[k]
                    u = U0[l] + k
                    a, wk = (0, T) if t < 2 else (S, S)
                    act.wait_ge(max_done, u + 1)
                    if u >= 2:
                        act.wait_ge(dif_done, u - 1)
                    for b in range(2):
                        act.activation(prob[:, u % 2, b, 0:wk], ps[:, 2 * (u % 2) + b, 0:wk], ACT.Exp,
                                       bias=nmax[:, u % 2, b:b + 1],
                                       accum_out=lsum[:, u % 2, b:b + 1]).then_inc(exp_done, 1)

                def unit_copy(k):
                    u = U0[l] + k
                    nk = 4 if us[k][0] < 2 else 2
                    act.wait_ge(tr_done, u + 1)
                    if u >= 2:
                        act.wait_ge(pv_done, u - 1)
                    act.activation(difT[:, u % 2, 0:nk, :], ps[:, 4 + u % 2, 0:nk * P].rearrange("p (a b) -> p a b", b=P),
                                   ACT.Copy).then_inc(difT_done, 1)

                def tile_square(t):
                    g = TB[l] + t
                    act.wait_ge(of_done, g + 1)
                    act.activation(sqk[:, g % 2, :], of[:, g % 2, :, :].rearrange("p h q -> p (h q)"), ACT.Square)\
                        .then_inc(osq_done, 1)

                def tile_rstd(t):
                    g = TB[l] + t
                    act.wait_ge(ostat, g + 1)
                    if t >= 1:
                        act.wait_ge(orstd, g)
                    else:
                        act.wait_ge(rq_done, 8 * (l + 1))
                    act.activation(lnk[:, :], ps[:, 6 + t % 2, :], ACT.Ln, bias=col("eps"), scale=1.0 / P)\
                        .then_inc(oln, 1)
                    act.wait_ge(oln, g + 1)
                    act.activation(rq[:, g % 2, :], lnk[:, :], ACT.Exp, scale=-0.5).then_inc(orstd, 1)

                def tile_high(t):
                    act.wait_ge(y_done, Y0[l] + 4 + t + 1)
                    act.activation(xh[:, 0:H, t * P:(t + 1) * P], of[:, (TB[l] + t) % 2, :, :], ACT.Copy)\
                        .then_inc(yh_done, 1)

                for k in range(len(us) + 3):
                    if k < len(us):
                        unit_exp(k)
                    if k == 0:
                        copy_v((2, 3))
                    if k == 5:
                        split_next(n0 + CV + VB - 1)
                    if 3 <= k <= len(us) + 2:
                        unit_copy(k - 3)
                    if k < 4:
                        act.wait_ge(y_done, Y0[l] + k + 1)
                        act.activation(xh[:, 4 + k, 0:w], cx[:, ysrc[k], 0:w], ACT.Copy).then_inc(yh_done, 1)
                    if tile_at(l, k, 8):
                        tile_square(k // H - 2)
                    if tile_at(l, k, 10):
                        tile_rstd(k // H - 2)
                    if tile_at(l, k, 11):
                        tile_high(k // H - 2)
                a, z = NT[l] - 2, NT[l] - 1
                tile_square(z)
                tile_rstd(a)
                tile_rstd(z)
                tile_high(a)
                tile_high(z)
                for d in range(OB - 1):
                    split_next(n0 + CV + VB + d)
                    if d >= 1:
                        square(3 * l + 2, d - 1)
                for d in (OB - 2, OB - 1):
                    square(3 * l + 2, d)
                split_next(n0 + CV + VB + OB - 1)
                norm(3 * l + 2)

            act.wait_ge(cols_in, 16)
            act.activation(cs[:, :], col("c", 0, DC * 2), ACT.Silu).then_inc(cs_done, 1)
            ln_exp_tables()
            for d in range(DC):
                square(0, d)
            split(0)
            split(1)
            norm(0)
            for l in range(DEPTH):
                ffn(l, 0)
                mixer(l)
                ffn(l, 2)

        @block.vector
        def _(dve):
            steps = [0]

            def own(ins):
                steps[0] += 1
                ins.then_inc(dve_step, 1)
                dve.wait_ge(dve_step, steps[0])

            def split(n, i=0, k=0):
                dve.wait_ge(hi_done, i * (4 * k) + (n + 1))
                dve.tensor_tensor(wlo[:, n % SPL, :, :].rearrange("p a b -> p (a b)"), raw[:, n % RAW, :],
                                  whi[:, n % SPL, :, :].rearrange("p a b -> p (a b)").bitcast(F32), ALU.subtract)\
                    .then_inc(lo_done, 1)

            def split_next(n, i=0, k=0):
                if n + SPL < NB:
                    split(n + SPL, i, k)

            def mod_pair(u, p, i=0):
                base = unit_steps(u)
                dve.wait_ge(wm_in[p % 2], i * (16 * PAIRS // 2) + 16 * (((u - START_UNITS) * PAIRS + p) // 2 + 1))
                for r in range(2):
                    c = 2 * p + r
                    for v in range(2):
                        sc = cs[:, 2 * c + v:2 * c + v + 1]
                        src, acc = wm[:, p % 2, r, :], macc[:, v, :]
                        if c == 0:
                            ins = dve.tensor_scalar(acc, src, sc, None, ALU.mult)
                        else:
                            dve.wait_ge(mod_acc, i * (2 * DC) + (base + 2 * c + v - 1))
                            ins = dve.scalar_tensor_tensor(acc, src, sc, acc, ALU.mult, ALU.add)
                        ins.then_inc(mod_acc, 1)
                dve.wait_ge(mod_acc, i * (2 * DC) + (base + 4 * p + 4))
                dve.sem_inc(wm_used, 1)

            def mod_columns(u, n=1, i=0, bank=5):
                dve.wait_ge(mod_sum, i + (u + n))
                a = COLS["b_mod"][0] + u * UC
                flat = modc[:, :, :, :].rearrange("p a b c -> p (a b c)")
                dve.tensor_tensor(flat[:, bass.ds(i * UC + u * UC, n * UC)], ps[:, bank, 0:n * UC],
                                  K[:, bass.ds(i * UC + a, n * UC)], ALU.add).then_inc(mod_col, n)

            def hidden(f, j, i, w):
                F0 = FC * f
                dve.wait_ge(silu_done, i * 2 + (F0 + j + 1))
                dve.tensor_tensor(af[:, j % 2, 0:w], sil[:, j % 2, 0:w], ps[:, 2 * (j % 2) + 1, 0:w], ALU.mult)\
                    .then_inc(mul_done, 1)

            def hidden_low(f, j, i, w):
                dve.wait_ge(ah_done, i * 2 + (FC * f + j + 1))
                dst = bass.ds(i * (2 * T) + j * T, w)
                dve.tensor_tensor(al[:, dst], af[:, j % 2, 0:w], ah[:, dst].bitcast(F32), ALU.subtract)\
                    .then_inc(al_done, 1)

            def gate_columns(m):
                l, st = divmod(m, 3)
                dve.wait_ge(mod_col, 2 * (N_MOD * l + 3 * st + 3))
                own(dve.tensor_scalar(gcol[:, m, :, :], modc[:, N_MOD * l + 3 * st + 2, :, :],
                                      1.0 if st == 1 else 0.5, None, ALU.mult))

            def update(m, d, bank):
                for s in range(streams(m)):
                    ins = dve.scalar_tensor_tensor(h[:, d, s * S:(s + 1) * S], ps[:, bank, s * S:(s + 1) * S],
                                                   gcol[:, m, d, s:s + 1], h[:, d, s * S:(s + 1) * S],
                                                   ALU.mult, ALU.add)
                ins.then_inc(h_done, 1)

            def add_square(m, d):
                w = width(m)
                g = DC * m + d
                dve.wait_ge(sq_done, g + 1)
                if d == 0:
                    if m > 0:
                        dve.wait_ge(stat_done, m)
                    dve.tensor_copy(ssq[:, 0:w], sq[:, g % 2, 0:w]).then_inc(ssq_done, 1)
                else:
                    dve.wait_ge(ssq_done, ADDED * m + d)
                    dve.tensor_tensor(ssq[:, 0:w], ssq[:, 0:w], sq[:, g % 2, 0:w], ALU.add).then_inc(ssq_done, 1)

            def norm(m):
                l, st = divmod(m, 3)
                w = width(m)
                dve.wait_ge(mod_col, 2 * (N_MOD * l + 3 * st + 2))
                own(dve.scalar_tensor_tensor(
                    acol[:, m, :, :].rearrange("p a b -> p (a b)"),
                    modc[:, N_MOD * l + 3 * st + 1, :, :].rearrange("p a b -> p (a b)"), 1.0,
                    col("norm_w", m * DC * 2, DC * 2), ALU.add, ALU.mult))
                def low(d, s):
                    g = xstep(m, d, s)
                    dve.wait_ge(xh_done, g)
                    dve.scalar_tensor_tensor(xl[:, d, s * S:(s + 1) * S], xt[:, (g - 1) % 4, :],
                                             modc[:, N_MOD * l + 3 * st, d, s:s + 1],
                                             xh[:, d, s * S:(s + 1) * S].bitcast(F32), ALU.add, ALU.subtract)\
                        .then_inc(xl_done, 1)

                todo = [(d, s) for s in range(streams(m)) for d in range(DC)]
                for q, (d, s) in enumerate(todo):
                    g = xstep(m, d, s)
                    if d == 0:
                        dve.wait_ge(rstd_done, 2 * m + s + 1)
                    if g > 4:
                        dve.wait_ge(xl_done, g - 4)
                    dve.scalar_tensor_tensor(xt[:, (g - 1) % 4, :], h[:, d, s * S:(s + 1) * S],
                                             acol[:, m, d, s:s + 1], rstd[:, s * S:(s + 1) * S],
                                             ALU.mult, ALU.mult).then_inc(xt_done, 1)
                    if q >= 2:
                        low(*todo[q - 2])
                low(*todo[-2])
                low(*todo[-1])

            def ffn(l, st):
                f = 2 * l + (st == 2)
                m = 3 * l + st
                n0 = PER_LAYER * l + (0 if st == 0 else FFN + MIX)
                w = width(m)
                u0, nu = UNIT_AT.get(f, (0, 0))

                def body(i, unit, columns, first=False):
                    for e in range(4):
                        split_next(n0 + e, i, 1)
                        if e % 2:
                            hidden(f, e // 2, i, w)
                        elif e or not first:
                            hidden_low(f, e // 2 - 1, i, w)
                        if e == 0 and columns:
                            mod_columns(u0 - 1, 1, i)
                        if unit:
                            mod_pair(u0, e, i)

                body(0, nu > 0, False, True)
                if nu:
                    with dve.Fori(1, nu) as i:
                        body(i, True, True)
                if 0 < nu < GU // 4:
                    with dve.Fori(nu, nu + 1) as i:
                        body(i, False, True)
                if nu + 1 < GU // 4:
                    with dve.Fori(nu + 1, GU // 4) as i:
                        body(i, False, False)
                hidden_low(f, -1, GU // 4, w)
                gate_columns(m)

                def half_out(hf, ds):
                    for d in ds:
                        if hf == 1 and d < 7:
                            dve.wait_ge(dn_done, 3 * f + d - 3)
                        else:
                            dve.wait_ge(block_done, n0 + GU + HALF * (hf + 1))
                        update(m, d, (4 if hf == 0 else 0) + d % 4)
                        if m + 1 < 6 and 4 * hf < d <= ADDED:
                            add_square(m + 1, d - 1)
                    if m + 1 < 6 and hf == 0:
                        add_square(m + 1, 3)

                for hf in range(2):
                    nd = n0 + GU + HALF * hf
                    split_next(nd)
                    with dve.Fori(0, (HALF - 3) // 4) as i:
                        for e in range(4):
                            split_next(nd + 1 + e, i, 1)
                    if hf == 0 and nu == GU // 4:
                        mod_columns(u0 + nu - 1, bank=0)
                    for b in (HALF - 2, HALF - 1):
                        if hf == 0:
                            split_next(nd + b)
                    half_out(hf, range(4 * hf, 4 * hf + 4))
                    for b in (HALF - 2, HALF - 1):
                        if hf == 1:
                            split_next(nd + b)
                if m + 1 < 6:
                    norm(m + 1)

            def conv(l, c):
                ns = ntile(l) // S
                sv = lambda j: cx[:, j, 0:ns * S].rearrange("p (s t) -> p s t", t=S)
                if c == 0:
                    own(dve.memset(cu[:, :, :, :], 0.0))
                cw = COLS["conv"][0] + (2 * l + c) * 3
                u = cu[:, c, 0:ns, :]
                y = cy[:, 0:ns, :]
                own(dve.tensor_tensor(u[:, :, 1:S + 1], sv(c), sv(2 + c), ALU.mult))
                own(dve.tensor_scalar(y, u[:, :, 1:S + 1], K[:, cw + 1:cw + 2], None, ALU.mult))
                own(dve.scalar_tensor_tensor(y, u[:, :, 0:S], K[:, cw:cw + 1], y, ALU.mult, ALU.add))
                own(dve.scalar_tensor_tensor(y, u[:, :, 2:S + 2], K[:, cw + 2:cw + 3], y, ALU.mult, ALU.add))
                dve.tensor_tensor(sv(4 + c), y, sv(4 + c), ALU.mult).then_inc(y_done, 1)
                dve.wait_ge(y_done, Y0[l] + c + 1)

            def pool_chunk(l, c):
                ns = ntile(l) // S
                sv = lambda j: cx[:, j, 0:ns * S].rearrange("p (s t) -> p s t", t=S)
                dve.memset(pad0[:, :, :], 0.0)
                own(dve.memset(pad1[:, :, :], 0.0))
                own(dve.tensor_copy(pad0[:, 0:ns, PADW:PADW + S], sv(6 + c)))
                src, dst = pad0, pad1
                for k, win in enumerate(WINDOWS[:2 * c + 2]):
                    a, b = (1, 0) if k == 0 else (win // 4, -(win // 4))
                    lo, hi = win // 2, PW - win // 2 + 1
                    own(dve.tensor_tensor(dst[:, 0:ns, lo:hi], src[:, 0:ns, lo - a:hi - a],
                                          src[:, 0:ns, lo - b:hi - b], ALU.add))
                    if k >= 2 * c:
                        g = k - 2 * c
                        pr = slice(64 * g, 64 * g + 64)
                        own(dve.tensor_tensor(box[pr, c, 0:ns, :], dst[pr, 0:ns, PADW:PADW + S], rc(c, ns)[pr],
                                              ALU.mult))
                    src, dst = dst, src
                dve.tensor_tensor(sv(c), box[:, c, 0:ns, :], sv(6 + c), ALU.subtract).then_inc(pooled_done, 1)

            def rc(c, ns):
                a = COLS["rcnt"][0] + c * S
                return K[:, a:a + S].rearrange("p (o t) -> p o t", o=1).broadcast_to([P, ns, S])

            def rope(l, b):
                qk = 8 * l + b
                wb = T if b < 4 else ntile(l)
                dve.wait_ge(rq_done, qk + 1)
                dve.scalar_tensor_tensor(kq[:, b, 0:wb], kq[:, b, 0:wb], col("kw", l) if b < 4 else qws[:, l:l + 1],
                                         rq[:, b % 2, 0:wb], ALU.mult, ALU.mult).then_inc(qk_used, 1)
                dve.wait_ge(qk_used, qk + 1)
                own(dve.stream_shuffle(shf[:, :], kq[:, b, 0:S], [(p + 16) % 32 for p in range(32)]))
                dve.tensor_tensor(kq[:, b, 0:S], kq[:, b, 0:S], col("cos", 0, S), ALU.mult)
                own(dve.tensor_tensor(rot[:, :], shf[:, :], col("sin", 0, S), ALU.mult))
                dve.tensor_tensor(kq[:, b, 0:S], kq[:, b, 0:S], rot[:, :], ALU.add).then_inc(qk_ready, 1)

            def lambda_sums():
                for l in range(DEPTH):
                    for b in range(2):
                        a = l * 4 * DH + 2 * b * DH
                        own(dve.tensor_tensor(lamt[:, b, :], col("lam", a, DH), col("lam", a + DH, DH), ALU.mult))
                        own(dve.tensor_reduce(lamc[:, l, b:b + 1], lamt[:, b, :], AX.X, ALU.add))
                dve.sem_inc(lam_red, 1)
                own(dve.tensor_scalar(qws[:, :], col("qw", 0, DEPTH), DH ** -0.5, None, ALU.mult))

            def lambda_ends():
                dve.wait_ge(lam_exp, 1)
                for l in range(DEPTH):
                    own(dve.tensor_tensor(lamc[:, l, 4:5], lamc[:, l, 3:4], lamc[:, l, 2:3], ALU.subtract))
                    own(dve.tensor_scalar(lamc[:, l, 5:6], lamc[:, l, 4:5], lam_init[l], None, ALU.subtract))
                    own(dve.tensor_scalar(lamc[:, l, 6:7], col("subln", l), 1.0 - lam_init[l], None, ALU.mult))

            def mixer(l):
                n0, w = B_win[l], ntile(l)
                for b in range(QKB + CB + VB - 1):
                    if b < CV + 2:
                        split_next(n0 + b)
                    if l == 0 and b == 0:
                        lambda_sums()
                    if l == 0 and b == QKB + 1:
                        lambda_ends()
                    if 1 <= b <= QKB:
                        rope(l, b - 1)
                    if l == 0 and QKB < b <= QKB + PAIRS:
                        mod_pair(MIX_UNIT, b - QKB - 1)
                    if l == 0 and b == QKB + PAIRS + 2:
                        mod_columns(MIX_UNIT)
                    if b in (CV - 3, CV - 2):
                        dve.wait_ge(evac, EV[l] + b)
                        conv(l, b - (CV - 3))
                    if b in (CV - 1, CV):
                        dve.wait_ge(evac, EV[l] + b)
                        pool_chunk(l, b - (CV - 1))
                    if b == CV + 2:
                        for c in range(2):
                            dve.wait_ge(pool_mm, 2 * l + c + 1)
                            dve.tensor_scalar(cx[:, c, 0:w], ps[:, c, 0:w], col("pscale", 2 * l + c), None, ALU.mult)\
                                .then_inc(y_done, 1)
                        dve.wait_ge(q_copied, l + 1)
                        dve.memset(kq[DH:P, H:2 * H, 0:w], 0.0).then_inc(q_ready, 1)
                        split_next(n0 + b)
                us = units(l)

                def unit_max(k):
                    t, _ = us[k]
                    u = U0[l] + k
                    wk = T if t < 2 else S
                    dve.wait_ge(score_done, u + 1)
                    if u >= 2:
                        dve.wait_ge(exp_done, 2 * (u - 1))
                    b0 = 2 * (u % 2)
                    dve.tensor_reduce(nmax[:, u % 2, :], ps[:, b0:b0 + 2, 0:wk], AX.X, ALU.max, negate=True)\
                        .then_inc(max_done, 1)

                def unit_dif(k):
                    t, _ = us[k]
                    u = U0[l] + k
                    wk = T if t < 2 else S
                    dve.wait_ge(exp_done, 2 * (u + 1))
                    own(dve.reciprocal(linv[:, u % 2, :], lsum[:, u % 2, :]))
                    dve.tensor_tensor(nlin[:, u % 2, :], linv[:, u % 2, 1:2], lamc[:, l, 5:6], ALU.mult)
                    if u >= 3:
                        dve.wait_ge(tr_done, u - 2)
                    own(dve.tensor_scalar(att[:, u % 3, 0:wk], prob[:, u % 2, 0, 0:wk], linv[:, u % 2, 0:1], None,
                                          ALU.mult))
                    dve.scalar_tensor_tensor(att[:, u % 3, 0:wk], prob[:, u % 2, 1, 0:wk], nlin[:, u % 2, :],
                                             att[:, u % 3, 0:wk], ALU.mult, ALU.add).then_inc(dif_done, 1)
                    dve.wait_ge(dif_done, u + 1)

                def tile_out(t):
                    g = TB[l] + t
                    dve.wait_ge(pv_done, U0[l] + H * (t + 1))
                    dve.tensor_copy(of[:, g % 2, :, :], ps[:, 6 + t % 2, :].rearrange("p (h q) -> p h q", h=H))\
                        .then_inc(of_done, 1)

                def tile_scale(t):
                    g = TB[l] + t
                    dve.wait_ge(orstd, g + 1)
                    flat = lambda a: a.rearrange("p h q -> p (h q)")
                    dve.scalar_tensor_tensor(flat(of[:, g % 2, :, :]), flat(of[:, g % 2, :, :]), lamc[:, l, 6:7],
                                             rq[:, g % 2, :], ALU.mult, ALU.mult).then_inc(y_done, 1)

                def tile_low(t):
                    dve.wait_ge(yh_done, Y0[l] + 4 + t + 1)
                    q = slice(t * P, (t + 1) * P)
                    dve.tensor_tensor(xl[:, 0:H, q], of[:, (TB[l] + t) % 2, :, :], xh32[:, 0:H, q], ALU.subtract)\
                        .then_inc(yl_done, 1)
                    dve.wait_ge(yl_done, Y0[l] + 4 + t + 1)

                for k in range(len(us) + 1):
                    if k < len(us):
                        unit_max(k)
                    if 1 <= k <= len(us):
                        unit_dif(k - 1)
                    if k == 6:
                        split_next(n0 + CV + VB - 1)
                    if tile_at(l, k, 8):
                        tile_out(k // H - 2)
                    if tile_at(l, k, 11):
                        tile_scale(k // H - 2)
                    if tile_at(l, k, 12):
                        tile_low(k // H - 3)
                a, z = NT[l] - 2, NT[l] - 1
                tile_out(z)
                tile_scale(a)
                tile_scale(z)
                tile_low(a)
                tile_low(z)
                m = 3 * l + 1
                gate_columns(m)
                for d in range(OB):
                    n = n0 + CV + VB + d
                    if d < OB - 1:
                        split_next(n)
                    dve.wait_ge(block_done, n + 1)
                    update(m, d, d % 4)
                    if 1 <= d <= ADDED:
                        add_square(m + 1, d - 1)
                split_next(n0 + CV + VB + OB - 1)
                norm(m + 1)

            dve.wait_ge(cols_in, 16)
            dve.memset(ps[:, 5, :], 0.0).then_inc(rows_zero, 1)
            for d in range(ADDED):
                add_square(0, d)
            split(0)
            dve.wait_ge(rows_done, 1)
            dve.tensor_copy(wm0_rows[:, :], ps[:, 5, :]).then_inc(rows_out, 1)
            split(1)
            dve.wait_ge(mod_sum, START_UNITS)
            turned = ps[:, 6, 0:START_UNITS * UC].rearrange("p (j u v) -> p u j v", u=START_UNITS, v=2)
            bias = col("b_mod", 0, START_UNITS * UC).rearrange("p (u j v) -> p u j v", u=START_UNITS, v=2)
            flat = modc[:, :, :, :].rearrange("p a b c -> p (a b c)")[:, 0:START_UNITS * UC]
            dve.tensor_tensor(flat.rearrange("p (u j v) -> p u j v", u=START_UNITS, v=2), turned, bias, ALU.add)\
                .then_inc(mod_col, START_UNITS)
            dve.wait_ge(mod_col, START_UNITS)
            norm(0)
            dve.wait_ge(cols2_in, 16)
            for l in range(DEPTH):
                ffn(l, 0)
                mixer(l)
                ffn(l, 2)

        @block.tensor
        def _(pe):
            def three(out_ap, hi_w, lo_w, hi_x, lo_x, start, stop):
                pe.matmul(out_ap, hi_w, hi_x, start=start, stop=False)
                pe.matmul(out_ap, hi_w, lo_x, start=False, stop=False)
                return pe.matmul(out_ap, lo_w, hi_x, start=False, stop=stop)

            def column_block(n, bank, w, i=0, k=0, ready=None, a=0, last=True, between=None):
                pe.wait_ge(lo_done, i * (4 * k) + (n + 1))
                for c in range(DC):
                    if c == 2 and between:
                        between()
                    if ready:
                        pe.wait_ge(*ready[c])
                    ins = three(ps[:, bank, a:w], whi[:, n % SPL, c, :], wlo[:, n % SPL, c, :],
                                xh[:, c, a:w], xl[:, c, a:w], c == 0, c == DC - 1)
                if last:
                    ins.then_inc(block_done, 1)

            def first_blocks(m, n):
                for s in range(streams(m)):
                    for q in range(2):
                        ready = {c: (xl_done, xstep(m, c, s)) for c in range(DC)} if q == 0 else None
                        column_block(n + q, q, (s + 1) * S, ready=ready, a=s * S, last=s == streams(m) - 1)

            def mod_start():
                pe.wait_ge(cs_done, 1)
                pe.wait_ge(rows_zero, 1)
                for c in range(DC):
                    if c % 2 == 0 or c == DC - 1:
                        pe.wait_ge(wm0_in[(c + 1) // 2], 16)
                    for u in range(START_UNITS):
                        ins = pe.matmul(ps[32 * u:32 * u + 2, 5, :], cs[:, 2 * c:2 * c + 2],
                                        wm0[:, c // 2, u, c % 2, :], start=c == 0, stop=c == DC - 1)
                ins.then_inc(rows_done, 1)
                pe.wait_ge(rows_out, 1)
                for j in range(HN // P):
                    ins = pe.matmul(ps[:, 6, 8 * j:8 * j + 8], wm0_rows[:, j * P:(j + 1) * P], col("sel", 0, 8),
                                    start=True, stop=True)
                ins.then_inc(mod_sum, START_UNITS)

            def mod_sums(u, i=0, bank=5):
                pe.wait_ge(mod_acc, i * (2 * DC) + unit_steps(u + 1))
                pe.wait_ge(mod_col, i + u)
                for c in range(HN // P):
                    for v in range(2):
                        ins = pe.matmul(ps[:, bank, 2 * c + v:2 * c + v + 1], macc[:, v, c * P:(c + 1) * P],
                                        col("one", 0, 1), start=True, stop=True)
                ins.then_inc(mod_sum, 1)

            def norm_stat(m):
                w = width(m)
                pe.wait_ge(ssq_done, ADDED * (m + 1))
                pe.matmul(ps[:, 4, 0:w], col("ones", 0, P), ssq[:, 0:w], start=True, stop=False)
                for d in (DC - 2, DC - 1):
                    pe.wait_ge(sq_done, DC * m + d + 1)
                    ins = pe.matmul(ps[:, 4, 0:w], col("ones", 0, P), sq[:, d % 2, 0:w], start=False, stop=d == DC - 1)
                ins.then_inc(stat_done, 1)

            def ffn(l, st):
                f = 2 * l + (st == 2)
                m = 3 * l + st
                n0 = PER_LAYER * l + (0 if st == 0 else FFN + MIX)
                w = width(m)
                u0, nu = UNIT_AT.get(f, (0, 0))
                F0 = FC * f

                def body(i, sums, first=False):
                    if first:
                        first_blocks(m, n0)
                    for e in range(2 if first else 0, 4):
                        if e % 2 == 0 and not first:
                            pe.wait_ge(mul_done, i * 2 + (F0 + e // 2 - 1))
                        column_block(n0 + e, e, w, i, 1,
                                     between=(lambda: mod_sums(u0 - 1, i)) if e == 1 and sums else None)

                body(0, False, True)
                if nu:
                    with pe.Fori(1, min(nu + 1, GU // 4)) as i:
                        body(i, True)
                if nu + 1 < GU // 4:
                    with pe.Fori(nu + 1, GU // 4) as i:
                        body(i, False)
                for hf in range(2):
                    nd = n0 + GU + HALF * hf
                    b0 = 4 if hf == 0 else 0

                    def down(b, i=0, k=0):
                        n = nd + b
                        pe.wait_ge(lo_done, i * (4 * k) + (n + 1))
                        if hf == 0:
                            pe.wait_ge(al_done, i * (8 * k) + (F0 + 2 * b + 2))
                        last = b == HALF - 1 and hf == 1
                        for r, d in [(r, d) for d in range(4) for r in range(2)] if last else \
                                [(r, d) for r in range(2) for d in range(4)]:
                            src = bass.ds(i * (8 * T * k) + (2 * b + r) * T, w)
                            ins = three(ps[:, b0 + d, 0:w], whi[:, n % SPL, 4 * r + d, :],
                                        wlo[:, n % SPL, 4 * r + d, :], ah[:, src], al[:, src],
                                        b == 0 and r == 0, b == HALF - 1 and r == 1)
                            if last and r == 1 and d < 3:
                                ins.then_inc(dn_done, 1)
                        ins.then_inc(block_done, 1)

                    if nu:
                        pe.wait_ge(mod_col, u0 + (min(nu, GU // 4 - 1) if hf == 0 else nu))
                    down(0)
                    with pe.Fori(0, (HALF - 3) // 4) as i:
                        for e in range(4):
                            down(1 + e, i, 1)
                    if hf == 0 and nu == GU // 4:
                        mod_sums(u0 + nu - 1, bank=0)
                    down(HALF - 2)
                    down(HALF - 1)
                if m + 1 < 6:
                    norm_stat(m + 1)

            def mixer(l):
                n0, w = B_win[l], ntile(l)
                m = 3 * l + 1

                def stat(b):
                    qk, wb = 8 * l + b, T if b < 4 else w
                    pe.wait_ge(sqk_done, qk + 1)
                    if b >= 2:
                        pe.wait_ge(rq_done, qk - 1)
                    pe.matmul(ps[:, 6 + b % 2, 0:wb], col("halves", 0, P), sqk[:, b % 2, 0:wb], start=True, stop=True)\
                        .then_inc(qk_stat, 1)

                first_blocks(m, n0)
                for b in range(1, QKB + CB):
                    if b >= 4:
                        pe.wait_ge(evac, EV[l] + b - 3)
                        if b - 4 < QKB:
                            pe.wait_ge(sqk_done, 8 * l + b - 3)
                    if b >= 2:
                        column_block(n0 + b, b % 4, T if b < 4 else w)
                    if 1 <= b <= QKB:
                        stat(b - 1)
                    if l == 0 and b == QKB + PAIRS + 1:
                        mod_sums(MIX_UNIT)
                pe.wait_ge(rq_done, 8 * (l + 1))
                if l == 0:
                    pe.wait_ge(mod_col, MIX_UNIT + 1)
                for b in range(VB):
                    n = n0 + CV + b
                    pe.wait_ge(lo_done, n + 1)
                    for r in range(2):
                        c = 2 * b + r
                        wh = whi[:, n % SPL, 4 * r:4 * r + 4, :].rearrange("p a b -> p (a b)")
                        wl = wlo[:, n % SPL, 4 * r:4 * r + 4, :].rearrange("p a b -> p (a b)")
                        for t in range(4):
                            ins = three(ps[:, 4 + t, :], xh[:, c, t * P:(t + 1) * P], xl[:, c, t * P:(t + 1) * P],
                                        wh, wl, c == 0, c == DC - 1)
                    ins.then_inc(block_done, 1)
                    if b in (1, 2):
                        c = b - 1
                        pe.wait_ge(pooled_done, 2 * l + c + 1)
                        pe.wait_ge(evac, EV[l] + 16)
                        pe.matmul(ps[:, c, 0:w], col("poolw", (2 * l + c) * P, P), pooled[:, c, 0:w],
                                  start=True, stop=True).then_inc(pool_mm, 1)
                us = units(l)
                pe.wait_ge(q_ready, l + 1)
                pe.wait_ge(q_zero, l + 1)
                pe.wait_ge(y_done, Y0[l] + 4)

                def scores(k):
                    t, hd = us[k]
                    u = U0[l] + k
                    a, wk = (0, T) if t < 2 else (S, S)
                    if k >= 2:
                        pe.wait_ge(exp_done, 2 * (u - 1))
                    for b, q in enumerate((kq[:, H + hd, :], cx[:, Z[hd], :])):
                        ins = pe.matmul(ps[:, 2 * (u % 2) + b, 0:wk], q[:, t * P:(t + 1) * P],
                                        kq[:, hd, a:a + wk], start=True, stop=True)
                    ins.then_inc(score_done, 1)

                def turn(k):
                    u = U0[l] + k
                    nk = 4 if us[k][0] < 2 else 2
                    pe.wait_ge(dif_done, u + 1)
                    if k == 0:
                        pe.wait_ge(evac, EV[l] + 20)
                    if k >= 2:
                        pe.wait_ge(difT_done, u - 1)
                    for j in range(nk):
                        ins = pe.transpose(ps[:, 4 + u % 2, j * P:(j + 1) * P], att[:, u % 3, j * P:(j + 1) * P],
                                           col("ident", 0, P))
                    ins.then_inc(tr_done, 1)

                def values(k):
                    t, hd = us[k]
                    u = U0[l] + k
                    k0, nk = (0, 4) if t < 2 else (2, 2)
                    pe.wait_ge(difT_done, u + 1)
                    if hd == 0 and t >= 2:
                        pe.wait_ge(orstd, TB[l] + t - 1)
                    for j in range(nk):
                        ins = pe.matmul(ps[:, 6 + t % 2, hd * P:(hd + 1) * P], vt[:, k0 + j, hd * P:(hd + 1) * P],
                                        difT[:, u % 2, j, :], start=(j == 0), stop=(j == nk - 1))
                    ins.then_inc(pv_done, 1)

                def tile_stat(t):
                    g = TB[l] + t
                    pe.wait_ge(osq_done, g + 1)
                    pe.matmul(ps[:, 6 + t % 2, :], col("ones", 0, P), sqk[:, g % 2, :], start=True, stop=True)\
                        .then_inc(ostat, 1)

                def out_part(d, chunks, a, b, start=False, stop=False, last=False):
                    n = n0 + CV + VB + d
                    pe.wait_ge(lo_done, n + 1)
                    for q, c in enumerate(chunks):
                        ins = three(ps[:, d, a:b], whi[:, n % SPL, c, :], wlo[:, n % SPL, c, :], xh[:, c, a:b],
                                    xl[:, c, a:b], start and q == 0, stop and q == len(chunks) - 1)
                    if last:
                        ins.then_inc(block_done, 1)

                def part(q):
                    out_part(q // 2, (4 + 2 * (q % 2), 5 + 2 * (q % 2)), 0, w, start=q % 2 == 0)

                for k in range(len(us) + 4):
                    if k < len(us):
                        scores(k)
                    if 3 <= k <= len(us) + 2:
                        turn(k - 3)
                    if 4 <= k <= len(us) + 3:
                        values(k - 4)
                    if tile_at(l, k, 9):
                        tile_stat(k // H - 2)
                    if k == len(us):
                        pe.wait_ge(yl_done, Y0[l] + 4)
                        pe.wait_ge(exp_done, 2 * (U0[l] + len(us) - 1))
                    if k in (len(us), len(us) + 1):
                        part(k - len(us))
                tile_stat(NT[l] - 2)
                part(2)
                tile_stat(NT[l] - 1)
                part(3)
                if l == 0:
                    pe.wait_ge(yl_done, Y0[l] + 4 + S // P)
                    for d in range(2):
                        out_part(d, range(4), 0, S)
                pe.wait_ge(yl_done, Y0[l] + 4 + NT[l])
                for d in range(2):
                    out_part(d, range(4), w - S, w, stop=True, last=True)
                for d in range(2, OB):
                    if d >= 4:
                        pe.wait_ge(h_done, DC * (3 * l + 1) + d - 3)
                    column_block(n0 + CV + VB + d, d % 4, w)
                norm_stat(3 * l + 2)

            pe.wait_ge(cols_in, 16)
            norm_stat(0)
            mod_start()
            for l in range(DEPTH):
                ffn(l, 0)
                mixer(l)
                ffn(l, 2)


def blocks_of(w, rows_per_block, col_chunks):
    k, n = w.shape
    a = w.reshape(k // (rows_per_block * P), rows_per_block, P, n // (col_chunks * P), col_chunks * P)
    a = a.transpose(3, 0, 2, 1, 4)
    return a.reshape(-1, P, BLK)


def kernel(x, c, ctx, c_ctx, norm_w, w_mod, b_mod, ffn1_w_gu, ffn1_w_down, ffn2_w_gu, ffn2_w_down,
           w_in, w_out, q_norm_w, k_norm_w, lambda_qk, subln_w, conv_w, pool_w, pool_scale):
    import concourse.bacc as bacc
    from concourse.bass_utils import run_bass_kernel_spmd

    f = lambda a: np.asarray(a)
    stream = []
    for l in range(DEPTH):
        def ffn_blocks(gu, dn):
            g = blocks_of(f(gu)[l], DC, 1)
            return [np.stack([g[:FC], g[FC:]], 1).reshape(-1, P, BLK), blocks_of(f(dn)[l], 2, 4)]
        stream += ffn_blocks(ffn1_w_gu, ffn1_w_down)
        wi = f(w_in)[l]
        W, C = 4 * P, 2 * P
        q, k, v, cb, cc, cxx, pu = (wi[:, a:b] for a, b in
                                    ((0, W), (W, 2 * W), (2 * W, 3 * W), (3 * W, 3 * W + C),
                                     (3 * W + C, 3 * W + 2 * C), (3 * W + 2 * C, 3 * W + 3 * C),
                                     (3 * W + 3 * C, 3 * W + 4 * C)))
        stream += [blocks_of(a, DC, 1) for a in (k, q, cc, cxx, cb, pu)] + [blocks_of(v, 2, 4)]
        stream += [blocks_of(f(w_out)[l], DC, 1)]
        stream += ffn_blocks(ffn2_w_gu, ffn2_w_down)
    wstream = np.concatenate(stream)
    assert wstream.shape[0] == NB
    wmod = np.ascontiguousarray(f(w_mod).reshape(DEPTH, PAIRS, 2, P, 2 * N_MOD, HN).transpose(0, 4, 1, 3, 2, 5)
                                .reshape(UNITS * PAIRS, P, 2 * HN))

    def two(a):
        a = a.reshape(-1, DC, P).transpose(2, 0, 1)
        return np.repeat(a[..., None], 2, -1).reshape(P, -1)

    nf = DH // 4
    inv = 10000.0 ** (-np.arange(nf, dtype=np.float32) / nf)
    t = np.arange(S)
    ang = np.stack([(t // GRID_W)[:, None] * inv, (t % GRID_W)[:, None] * inv], 1).astype(np.float32)
    cos = np.repeat(np.cos(ang)[:, :, None], 2, 2).reshape(S, DH).T
    sin = np.stack([-np.sin(ang), np.sin(ang)], 2).reshape(S, DH).T
    win = np.repeat(np.array(WINDOWS), DH)[:, None]
    cnt = np.minimum(t + win // 2, S) - np.maximum(t - win // 2, 0)
    pw = np.zeros((DEPTH, 2, P, P), np.float32)
    for g in range(4):
        a = slice(64 * (g % 2), 64 * (g % 2) + 64)
        pw[:, g // 2, a, a] = f(pool_w)[:, g]
    pieces = {
        "c": np.stack([f(c)[0], f(c_ctx)], -1).reshape(DC, P, 2).transpose(1, 0, 2).reshape(P, -1),
        "norm_w": two(f(norm_w)),
        "b_mod": two(f(b_mod)),
        "qw": np.tile(f(q_norm_w).T, (2, 1)),
        "kw": np.tile(f(k_norm_w).T, (2, 1)),
        "subln": f(subln_w).T,
        "conv": f(conv_w).reshape(DEPTH, 3, 2, P).transpose(3, 0, 2, 1).reshape(P, -1),
        "pscale": f(pool_scale).reshape(DEPTH * 2, P).T,
        "lam": np.broadcast_to(f(lambda_qk).reshape(1, -1), (P, DEPTH * 4 * DH)),
        "eps": np.full((P, 1), EPS),
        "one": np.ones((P, 1)),
        "sel": np.stack([np.arange(P) == 32 * u + v for u in range(4) for v in range(2)], 1),
        "cos": np.tile(cos, (2, 1)),
        "sin": np.tile(sin, (2, 1)),
        "rcnt": (1.0 / cnt).reshape(2, P, S).transpose(1, 0, 2).reshape(P, -1),
        "ones": np.ones((P, P)),
        "halves": np.kron(np.eye(2), np.ones((DH, DH))),
        "ident": np.eye(P),
        "poolw": pw.transpose(2, 0, 1, 3).reshape(P, -1),
    }
    cols = np.zeros((P, NCOL), np.float32)
    for name, (a, n) in COLS.items():
        cols[:, a:a + n] = pieces[name]
    x_t = np.ascontiguousarray(np.concatenate([f(x)[0], f(ctx)[0]]).T)

    nc = bacc.Bacc("TRN2", target_bir_lowering=False, num_devices=1)
    arrays = {"wstream": wstream, "wmod": wmod, "cols": cols, "x_t": x_t}
    aps = {n: nc.dram_tensor(n, a.shape, F32, kind="ExternalInput").ap() for n, a in arrays.items()}
    out = nc.dram_tensor("out_t", (D, S), F32, kind="ExternalOutput").ap()
    program(nc, aps["wstream"], aps["wmod"], aps["cols"], aps["x_t"], out)
    r = run_bass_kernel_spmd(nc, [arrays], core_ids=[0])
    return np.ascontiguousarray(r.results[0]["out_t"].T)[None]
```
